# Optimizing a Trainium2 kernel written in Bass

```python
import jax, jax.numpy as jnp
from jax import lax
import numpy as np

D_MODEL = 1024
BATCH = 1
SEQ = 256
DEPTH = 1
DEC_BATCH = 8
DEC_SEQ = 1
PAST_LEN = 1024
PAGE_SIZE = 128

H_A = 8
DH_A = 64
Q_BLOCK = 128
FORGET_BIAS = 7.0
H_B = 4
DK_B = 64
DV_B = 128
GLA_RANK = 16
GLA_TAU = 16.0
GLA_CHUNK = 64
N_EXPERTS = 32
TOP_K = 4
D_FF = 1024
SWIGLU_LIMIT = 7.0
SWIGLU_ALPHA = 1.702
MOE_BLOCK = 128
RMS_EPS = 1e-6

W_A = H_A * DH_A
WK_B = H_B * DK_B
WV_B = H_B * DV_B
IN_SIZES = (W_A, W_A, W_A, H_A, WK_B, WK_B, WV_B, WV_B, GLA_RANK, D_MODEL, D_MODEL)
D_IN = sum(IN_SIZES)

kernel_name = "fox_gla_parallel_moe_adaln_step"

def rmsnorm(x, g):
    xf = x.astype(jnp.float32)
    y = xf * lax.rsqrt(jnp.mean(xf * xf, axis=-1, keepdims=True) + RMS_EPS)
    return (y * g.astype(jnp.float32)).astype(x.dtype)

def split_cols(z, sizes):
    idx = np.cumsum(np.array(sizes))[:-1].tolist()
    return jnp.split(z, idx, axis=-1)

def fox_attention(q, k, v, cq, ck, q_pos, k_pos):
    B, T, H, Dh = q.shape
    qbs = Q_BLOCK if T % Q_BLOCK == 0 else T
    nb = T // qbs
    scale = Dh ** -0.5
    q_blocks = q.reshape(B, nb, qbs, H, Dh).transpose(1, 0, 2, 3, 4)
    cq_blocks = cq.astype(jnp.float32).reshape(B, nb, qbs, H).transpose(1, 0, 3, 2)
    pos_blocks = q_pos.reshape(nb, qbs)
    ck_t = jnp.swapaxes(ck.astype(jnp.float32), 1, 2)

    def one_block(args):
        qi, cqi, pi = args
        s = jnp.einsum('bqhd,bshd->bhqs', qi, k).astype(jnp.float32) * scale
        s = s + cqi[..., :, None] - ck_t[..., None, :]
        causal = k_pos[None, :] <= pi[:, None]
        s = jnp.where(causal, s, -jnp.inf)
        p = jax.nn.softmax(s, axis=-1)
        return jnp.einsum('bhqs,bshd->bqhd', p.astype(v.dtype), v)

    o = lax.map(one_block, (q_blocks, cq_blocks, pos_blocks))
    return o.transpose(1, 0, 2, 3, 4).reshape(B, T, H, Dh)

def gla_recurrence(q, k, v, log_a, s0):
    B, T, H, K = q.shape
    V = v.shape[-1]
    C = GLA_CHUNK if T % GLA_CHUNK == 0 else T
    n = T // C

    def chunks(z):
        return z.reshape(B, n, C, H, z.shape[-1]).transpose(1, 0, 3, 2, 4).astype(jnp.float32)

    tril = jnp.tril(jnp.ones((C, C), dtype=bool))

    def step(S, inp):
        qc, kc, vc, ac = inp
        b = jnp.cumsum(ac, axis=2)
        diff = b[:, :, :, None, :] - b[:, :, None, :, :]
        decay = jnp.exp(jnp.where(tril[:, :, None], diff, -jnp.inf))
        A = jnp.einsum('bhtk,bhsk,bhtsk->bhts', qc, kc, decay)
        o = jnp.einsum('bhts,bhsv->bhtv', A, vc) + jnp.einsum('bhtk,bhkv->bhtv', qc * jnp.exp(b), S)
        b_last = b[:, :, -1, :]
        S_new = jnp.exp(b_last)[..., None] * S + jnp.einsum(
            'bhsk,bhsv->bhkv', kc * jnp.exp(b_last[:, :, None, :] - b), vc)
        return S_new, o

    S_fin, o = lax.scan(step, s0.astype(jnp.float32), (chunks(q), chunks(k), chunks(v), chunks(log_a)))
    o = o.transpose(1, 0, 3, 2, 4).reshape(B, T, H, V)
    return o, S_fin

def expert_ffn(xb, w_gu, b_gu, w_d, b_d):
    gu = xb @ w_gu + b_gu
    gate, up = jnp.split(gu, 2, axis=-1)
    gate = jnp.minimum(gate, SWIGLU_LIMIT)
    up = jnp.clip(up, -SWIGLU_LIMIT, SWIGLU_LIMIT)
    glu = gate * jax.nn.sigmoid(SWIGLU_ALPHA * gate)
    return ((up + 1) * glu) @ w_d + b_d

def moe(h, w_router, b_router, w_gu, b_gu, w_d, b_d):
    lead = h.shape[:-1]
    D = h.shape[-1]
    x = h.reshape(-1, D)
    N = x.shape[0]
    NK = N * TOP_K
    logits = (x @ w_router).astype(jnp.float32) + b_router.astype(jnp.float32)
    top_v, top_e = lax.top_k(logits, TOP_K)
    gates = jax.nn.softmax(top_v, axis=-1)
    flat_e = top_e.reshape(-1).astype(jnp.int32)
    order = jnp.argsort(flat_e)
    sorted_e = flat_e[order]
    counts = jnp.bincount(flat_e, length=N_EXPERTS).astype(jnp.int32)
    padded = (counts + MOE_BLOCK - 1) // MOE_BLOCK * MOE_BLOCK
    pad_end = jnp.cumsum(padded).astype(jnp.int32)
    pad_start = pad_end - padded
    grp_start = jnp.cumsum(counts).astype(jnp.int32) - counts
    rank = jnp.arange(NK, dtype=jnp.int32) - grp_start[sorted_e]
    dest_sorted = (pad_start[sorted_e] + rank).astype(jnp.int32)
    dest = jnp.zeros((NK,), jnp.int32).at[order].set(dest_sorted)
    n_blocks = -(-(NK + N_EXPERTS * (MOE_BLOCK - 1)) // MOE_BLOCK)
    R = n_blocks * MOE_BLOCK
    row_tok = jnp.zeros((R,), jnp.int32).at[dest].set(jnp.arange(NK, dtype=jnp.int32) // TOP_K)
    block_start = jnp.arange(n_blocks, dtype=jnp.int32) * MOE_BLOCK
    block_e = jnp.minimum(jnp.searchsorted(pad_end, block_start, side='right'), N_EXPERTS - 1)
    x_rows = x[row_tok].reshape(n_blocks, MOE_BLOCK, D)

    def run_block(args):
        xb, e = args
        return expert_ffn(xb, w_gu[e], b_gu[e], w_d[e], b_d[e])

    y_rows = lax.map(run_block, (x_rows, block_e)).reshape(R, D)
    y_sel = y_rows[dest].reshape(N, TOP_K, D)
    y = jnp.einsum('nk,nkd->nd', gates.astype(y_sel.dtype), y_sel)
    return y.reshape(*lead, D)

def decoder_layer(x, c, past, lw):
    (g_mix, g_ffn, w_ada, b_ada, w_in, b_f, w_alpha, b_alpha, g_gla,
     w_branch, w_o, w_router, b_router, w_gu, b_gu, w_d, b_d) = lw
    B, T, _ = x.shape
    mod = (jax.nn.silu(c) @ w_ada + b_ada)[:, None, :]
    sh1, sc1, gt1, sh2, sc2, gt2 = jnp.split(mod, 6, axis=-1)

    h = rmsnorm(x, g_mix) * (1 + sc1) + sh1
    qa, ka, va, fa, qb, kb, vb, rb, alr, ga, gb = split_cols(h @ w_in, IN_SIZES)
    qa = qa.reshape(B, T, H_A, DH_A)
    ka = ka.reshape(B, T, H_A, DH_A)
    va = va.reshape(B, T, H_A, DH_A)
    logf = jax.nn.log_sigmoid((fa + b_f).astype(jnp.float32))
    cum_new = jnp.cumsum(logf, axis=1)
    if past is None:
        pos = jnp.arange(T, dtype=jnp.int32)
        o_a = fox_attention(qa, ka, va, cum_new, cum_new, pos, pos)
        s0 = jnp.zeros((B, H_B, DK_B, DV_B), jnp.float32)
    else:
        k_past, v_past, logf_past, s0 = past
        P = k_past.shape[1]
        lp = logf_past.astype(jnp.float32)
        suffix = lax.cumsum(lp, axis=1, reverse=True) - lp
        ck = jnp.concatenate([-suffix, cum_new], axis=1)
        k_all = jnp.concatenate([k_past.astype(ka.dtype), ka], axis=1)
        v_all = jnp.concatenate([v_past.astype(va.dtype), va], axis=1)
        q_pos = P + jnp.arange(T, dtype=jnp.int32)
        k_pos = jnp.arange(P + T, dtype=jnp.int32)
        o_a = fox_attention(qa, k_all, v_all, cum_new, ck, q_pos, k_pos)

    log_a = jax.nn.log_sigmoid((alr @ w_alpha + b_alpha).astype(jnp.float32)) / GLA_TAU
    o_b, s_new = gla_recurrence((qb * DK_B ** -0.5).reshape(B, T, H_B, DK_B),
                                kb.reshape(B, T, H_B, DK_B),
                                vb.reshape(B, T, H_B, DV_B),
                                log_a.reshape(B, T, H_B, DK_B), s0)
    o_b = rmsnorm(o_b.astype(x.dtype), g_gla.reshape(H_B, DV_B))
    o_b = o_b.reshape(B, T, WV_B) * jax.nn.silu(rb)

    y_a = o_a.reshape(B, T, W_A) @ w_branch[:W_A]
    y_b = o_b @ w_branch[W_A:]
    mixed = (jax.nn.sigmoid(ga) * y_a + jax.nn.sigmoid(gb) * y_b) @ w_o
    x = x + gt1 * mixed

    h2 = rmsnorm(x, g_ffn) * (1 + sc2) + sh2
    x = x + gt2 * moe(h2, w_router, b_router, w_gu, b_gu, w_d, b_d)
    return x, ka, va, logf, s_new

def setup_inputs(seed: int = 0) -> dict:
    key = jax.random.key(seed)
    ks = jax.random.split(key, 40)
    n_pages = PAST_LEN // PAGE_SIZE
    n_phys = (DEC_BATCH * n_pages * 5) // 4
    f32 = jnp.float32

    def nrm(k, shape, scale):
        return jax.random.normal(k, shape, f32) * scale

    L = DEPTH
    d = D_MODEL
    inputs = {
        "x_prompt": nrm(ks[0], (BATCH, SEQ, d), 1.0),
        "x_sample": nrm(ks[1], (DEC_BATCH, DEC_SEQ, d), 1.0),
        "c_prompt": nrm(ks[2], (BATCH, d), 1.0),
        "c_sample": nrm(ks[3], (DEC_BATCH, d), 1.0),
        "cache_k": nrm(ks[4], (L, n_phys, PAGE_SIZE, H_A, DH_A), 1.0),
        "cache_v": nrm(ks[5], (L, n_phys, PAGE_SIZE, H_A, DH_A), 1.0),
        "cache_logf": jax.nn.log_sigmoid(FORGET_BIAS + nrm(ks[6], (L, n_phys, PAGE_SIZE, H_A), 1.0)),
        "state_gla": nrm(ks[7], (L, DEC_BATCH, H_B, DK_B, DV_B), 0.5),
        "page_table": jax.random.permutation(ks[8], n_phys)[:DEC_BATCH * n_pages]
                          .reshape(DEC_BATCH, n_pages).astype(jnp.int32),
        "g_mix": 1.0 + nrm(ks[9], (L, d), 0.01),
        "g_ffn": 1.0 + nrm(ks[10], (L, d), 0.01),
        "g_final": 1.0 + nrm(ks[11], (d,), 0.01),
        "w_ada": nrm(ks[12], (L, d, 6 * d), 0.5 * d ** -0.5),
        "b_ada": nrm(ks[13], (L, 6 * d), 0.01),
        "w_in": nrm(ks[14], (L, d, D_IN), d ** -0.5),
        "b_f": FORGET_BIAS + nrm(ks[15], (L, H_A), 0.5),
        "w_alpha": nrm(ks[16], (L, GLA_RANK, WK_B), GLA_RANK ** -0.5),
        "b_alpha": nrm(ks[17], (L, WK_B), 0.5),
        "g_gla": 1.0 + nrm(ks[18], (L, WV_B), 0.01),
        "w_branch": nrm(ks[19], (L, W_A + WV_B, d), W_A ** -0.5),
        "w_o": nrm(ks[20], (L, d, d), d ** -0.5),
        "w_router": nrm(ks[21], (L, d, N_EXPERTS), d ** -0.5),
        "b_router": nrm(ks[22], (L, N_EXPERTS), 0.01),
        "w_gu": nrm(ks[23], (L, N_EXPERTS, d, 2 * D_FF), d ** -0.5),
        "b_gu": nrm(ks[24], (L, N_EXPERTS, 2 * D_FF), 0.01),
        "w_d": nrm(ks[25], (L, N_EXPERTS, D_FF, d), D_FF ** -0.5),
        "b_d": nrm(ks[26], (L, N_EXPERTS, d), 0.01),
    }
    return inputs

def reference(x_prompt, x_sample, c_prompt, c_sample, cache_k, cache_v, cache_logf, state_gla,
              page_table, g_mix, g_ffn, g_final, w_ada, b_ada, w_in, b_f, w_alpha, b_alpha, g_gla,
              w_branch, w_o, w_router, b_router, w_gu, b_gu, w_d, b_d):
    n_pages = PAST_LEN // PAGE_SIZE
    db = x_sample.shape[0]
    xp = x_prompt
    xs = x_sample
    kp_l, vp_l, fp_l, sp_l = [], [], [], []
    ks_l, vs_l, fs_l, ss_l = [], [], [], []
    for layer in range(DEPTH):
        lw = (g_mix[layer], g_ffn[layer], w_ada[layer], b_ada[layer], w_in[layer], b_f[layer],
              w_alpha[layer], b_alpha[layer], g_gla[layer], w_branch[layer], w_o[layer],
              w_router[layer], b_router[layer], w_gu[layer], b_gu[layer], w_d[layer], b_d[layer])
        xp, kp, vp, fp, sp = decoder_layer(xp, c_prompt, None, lw)
        k_past = cache_k[layer][page_table].reshape(db, n_pages * PAGE_SIZE, H_A, DH_A)
        v_past = cache_v[layer][page_table].reshape(db, n_pages * PAGE_SIZE, H_A, DH_A)
        f_past = cache_logf[layer][page_table].reshape(db, n_pages * PAGE_SIZE, H_A)
        xs, ksm, vsm, fsm, ssm = decoder_layer(xs, c_sample, (k_past, v_past, f_past, state_gla[layer]), lw)
        kp_l.append(kp); vp_l.append(vp); fp_l.append(fp); sp_l.append(sp)
        ks_l.append(ksm); vs_l.append(vsm); fs_l.append(fsm); ss_l.append(ssm)
    y_prompt = rmsnorm(xp, g_final)
    y_sample = rmsnorm(xs, g_final)
    k_prompt = jnp.stack(kp_l, axis=0)
    v_prompt = jnp.stack(vp_l, axis=0)
    logf_prompt = jnp.stack(fp_l, axis=0)
    gla_prompt = jnp.stack(sp_l, axis=0)
    k_sample = jnp.stack(ks_l, axis=0)
    v_sample = jnp.stack(vs_l, axis=0)
    logf_sample = jnp.stack(fs_l, axis=0)
    gla_sample = jnp.stack(ss_l, axis=0)
    return (y_prompt, y_sample, k_prompt, v_prompt, logf_prompt, gla_prompt,
            k_sample, v_sample, logf_sample, gla_sample)


_drawn_inputs = setup_inputs


def setup_inputs(seed=0):
    import zlib

    import numpy as np

    out = dict(_drawn_inputs(seed))
    spreads = {}
    factors = {'cache_k': 6.706,
     'cache_v': 5.467,
     'cache_logf': 200.0,
     'g_mix': 3.969,
     'g_ffn': 13.88,
     'g_final': 187.055,
     'g_gla': 30.05,
     'b_router': 24.821,
     'b_gu': 100.561,
     'b_d': 200.0}
    for name, (base, spread) in spreads.items():
        noise = np.random.default_rng([zlib.crc32(name.encode()), seed]).standard_normal(out[name].shape)
        drawn = base * np.exp(spread * noise) if base else spread * noise
        out[name] = __import__('jax').numpy.asarray(drawn.astype(out[name].dtype))
    for name, factor in factors.items():
        out[name] = (out[name] * factor).astype(out[name].dtype)
    return out
```

```python
from contextlib import ExitStack

import concourse.bass as bass
import numpy as np
from concourse import mybir

F32 = mybir.dt.float32
I32 = mybir.dt.int32
U32 = mybir.dt.uint32
ALU = mybir.AluOpType
ACT = mybir.ActivationFunctionType
AX_X = mybir.AxisListType.X

P = 128
D = 1024
KT = D // P
TP = 256
NS = 8
T = TP + NS
HA, DH = 8, 64
WA = HA * DH
HB, DK, DV = 4, 64, 128
CH = 64
NCH = TP // CH
PAGES, PAGE, N_PHYS = 8, 128, 80
NE, TOPK, FF = 32, 4, 1024
CAP = 64
PAIRS = NE // 2
MAX_ROUNDS = -(-T // CAP)
EPS = 1e-6
LIMIT, ALPHA = 7.0, 1.702
SCALE = DH ** -0.5
TAU = 16.0
NEG = -1e30
EXP_CLAMP = 80.0

QA, KA, VA, FA = 0, 512, 1024, 1536
QB, KB, VB = 1544, 1800, 2056
RB, ALR, GA, GB = 2568, 3080, 3096, 4120

TOK_TILES = [(0, 128), (128, 128), (256, 8)]

ITEMS = (["ada0", "ada1", "ada2", "ada3", "qa", "ka", "va", "fqk", "K0", "K1", "vb", "K2", "K3", "rb"]
         + [f"K{b}" for b in range(4, NS)] + ["state"] + [f"V{b}" for b in range(NS)]
         + ["ga0", "ada4", "ada5", "ga1", "ada6", "ada7", "gb0", "ada8", "ada9", "gb1", "ada10", "ada11"]
         + ["wb0", "wb1", "wo0", "wo1"])
WIN = {"qa": (QA, 512), "ka": (KA, 512), "va": (VA, 512), "fqk": (FA, 520), "vb": (VB, 512),
       "rb": (RB, 528), "ga0": (GA, 512), "ga1": (GA + 512, 512), "gb0": (GB, 512), "gb1": (GB + 512, 512)}
SLOTS = 6
SLOT = 528 * KT
EXPERT_SLOTS = [(len(ITEMS) + s) % SLOTS for s in range(SLOTS)]

VEC_ROWS = {"b_ada": (0, 48), "g_mix": (48, 8), "g_ffn": (56, 8), "g_final": (64, 8), "g_gla": (72, 4),
            "b_alpha": (76, 2)}
N_VEC = 78
N_SMALL = 720


def decoder_step(nc, x_prompt, x_sample, c_prompt, c_sample, cache_k, cache_v, cache_logf, state_gla,
                 page_table, g_mix, g_ffn, g_final, w_ada, b_ada, w_in, b_f, w_alpha, b_alpha, g_gla,
                 w_branch, w_o, w_router, b_router, w_gu, b_gu, w_d, b_d,
                 y_prompt, y_sample, k_prompt, v_prompt, logf_prompt, gla_prompt,
                 k_sample, v_sample, logf_sample, gla_sample):
    with ExitStack() as ctx:
        def sb(name, shape, dt=F32):
            return ctx.enter_context(nc.sbuf_tensor(name, shape, dt))

        def sem(name):
            return ctx.enter_context(nc.semaphore(name))

        ps = ctx.enter_context(nc.psum_tensor("ps", [P, 8, 512], F32))
        ring = sb("ring", [P, SLOTS, SLOT])
        ident = sb("ident", [P, P])
        ones = sb("ones", [P, P])
        before = sb("before", [P, P])
        after = sb("after", [P, P])
        causal = sb("causal", [P, 2 * P])
        keep_s_le_t = sb("keep_s_le_t", [CH, CH])
        slots_iota = sb("slots_iota", [P, CAP])
        vecT = sb("vecT", [P, N_VEC])
        b_f_col = sb("b_f_col", [HA, 1])
        w_alpha_sb = sb("w_alpha_sb", [16, 256])
        pages_row = sb("pages_row", [1, NS * PAGES], I32)
        pages_col = sb("pages_col", [NS * PAGES, 1], I32)
        modT = sb("modT", [P, 48, 9])
        cT = sb("cT", [P, KT, 9])
        gain1 = sb("gain1", [P, KT, 9])
        gain2 = sb("gain2", [P, KT, 9])
        xT = sb("xT", [P, KT, T])
        hT = sb("hT", [P, KT, T])
        tok = sb("tok", [P, 3, D])
        zone = sb("zone", [P, 10560])
        k_tok = sb("k_tok", [P, 3, WA])
        v_tok = sb("v_tok", [P, 2, WA])
        oT = sb("oT", [P, 4, T])
        attn = sb("attn", [P, 4, 384])
        gla_S = sb("gla_S", [P, NCH, 2, DV])
        neg_cum = sb("neg_cum", [P, T])
        f_tok = sb("f_tok", [P, 5, HA])
        dec_scores = sb("dec_scores", [P, HA * NS, PAGES])
        small = sb("small", [P, N_SMALL])

        def part(base, rows, off, *dims):
            n = int(np.prod(dims))
            ap = base[rows, off:off + n]
            if len(dims) == 2:
                return ap.rearrange("p (a b) -> p a b", b=dims[1])
            if len(dims) == 3:
                return ap.rearrange("p (a b c) -> p a b c", b=dims[1], c=dims[2])
            return ap

        ALLP = slice(0, P)
        qT = part(zone, ALLP, 0, 4, T)
        kT = part(zone, ALLP, 1056, 4, T)
        vT = part(zone, ALLP, 2112, 4, T)
        qbT = part(zone, ALLP, 3168, 2, T)
        kbT = part(zone, ALLP, 3696, 2, T)
        vbT = part(zone, ALLP, 4224, 4, T)
        rbT = part(zone, ALLP, 5280, 4, T)
        gaT = part(zone, ALLP, 6336, KT, T)
        gbT = part(zone, ALLP, 8448, KT, T)
        past_lf = part(zone, ALLP, 1056, HA * NS, PAGES)
        past_suffix = part(zone, ALLP, 1568, HA * NS, PAGES)
        vec_rows = part(zone, slice(0, N_VEC), 0, P)
        k_new_rows, v_new_rows = k_tok[0:NS, 2, :], k_tok[32:32 + NS, 2, :]
        fT = part(zone, slice(0, HA), 6336, T)
        f_nabs = part(zone, slice(0, HA), 7888, T)
        alrT = part(zone, slice(0, 16), 7888, T)
        al_x = part(zone, ALLP, 6336, 2, T)
        al_d = part(zone, ALLP, 6864, 2 * NCH, CH)
        al_b = part(zone, ALLP, 7376, 2 * NCH, CH)
        e_q = part(zone, ALLP, 7888, 2 * NCH, CH)
        e_k = part(zone, ALLP, 8400, 2 * NCH, CH)
        e_b = part(zone, ALLP, 8912, 2 * NCH, CH)
        q_rows = part(zone, slice(0, NS), 9936, WA)
        qe = part(zone, ALLP, 9424, 2, 2 * NCH, CH)
        kd_tok = tok[0:CH, 0, :].rearrange("p (i c k) -> p i c k", i=2, c=NCH)
        vb_tok = tok[0:CH, 1:3, :].rearrange("p a (c v) -> p (a c) v", v=HB * DV)
        c_rows = hT[0:9, :, :].rearrange("p a b -> p (a b)")[:, 0:D]
        junk = hT[:, :, :].rearrange("p a b -> p (a b)")[:, D + 64:2 * D + 64]
        rstd_diag = attn[:, 0, :].rearrange("p (t c) -> p t c", t=3)
        al_nabs = part(zone, ALLP, 8400, 2, T)
        ob_sq = part(zone, ALLP, 6336, 4, T)
        ob_rs = part(zone, ALLP, 7888, 4, T)
        obT = k_tok[:, :, :].rearrange("p a b -> p (a b)")[:, 0:4 * T].rearrange("p (h t) -> p h t", h=4)
        attn_flat = attn[:, :, :].rearrange("p a b -> p (a b)")
        A_T = attn_flat[0:CH, 0:1024].rearrange("p (i f c t) -> p i f (c t)", i=2, f=2, c=NCH)
        vb_rows = attn_flat[0:NS, 1024:1536]
        lf_rows = gla_S[0:NS * PAGES, :, :, :].rearrange("p a b c -> p (a b c)")
        acc = part(zone, ALLP, 0, KT, T)
        xg = part(zone, ALLP, 2112, KT, 2 * CAP)
        gate_v = part(zone, slice(0, CAP), 3136, FF)
        hid = part(zone, slice(0, CAP), 4160, FF)
        b_d_sb = part(zone, slice(0, NE), 5184, D)
        pick = part(zone, ALLP, 6336, 3, 2 * CAP)
        put = part(zone, ALLP, 6720, 3, 2 * CAP)
        putT = part(zone, ALLP, 7104, T)
        expert_row = part(zone, slice(0, NE), 7368, 2, CAP)
        b_gu_rows = part(zone, slice(0, NE), 7496, 2 * FF)
        place = part(zone, ALLP, 9928, 3, NE)
        gates = part(zone, ALLP, 10024, 3, NE)
        w_r = part(zone, ALLP, 10120, KT, NE)
        gatesT = part(zone, slice(0, NE), 9544, T)
        sq_zone = part(zone, ALLP, 0, KT, T)
        hidT = oT[:, :, :].rearrange("p a b -> p (a b)")[:, 0:KT * CAP].rearrange("p (k c) -> p k c", c=CAP)
        sig_v = k_tok[0:CAP, :, :].rearrange("p a b -> p (a b)")[:, 0:FF]
        ye_tok = v_tok[:, :, :].rearrange("p a b -> p (a b)")

        at = [0]

        def tiny(rows, *dims):
            off = at[0]
            at[0] += int(np.prod(dims))
            assert at[0] <= N_SMALL, at[0]
            return part(small, slice(0, rows), off, *dims)

        ssq = tiny(P, 3)
        rstd = tiny(P, 3)
        row_max = tiny(P, 16)
        row_sum = tiny(P, 16)
        row_inv = tiny(P, 16)
        b_last = tiny(P, 2 * NCH)
        la_new = tiny(P, 2, NS)
        qb_new = tiny(P, 2, NS, 2)
        qk_new = tiny(P, HA, NS)
        s_new = tiny(P, HA, NS)
        f_diag = tiny(NS, HA, NS)
        f_new = tiny(P, HA, NS)
        dec_max = tiny(P, HA * NS)
        dec_top = tiny(P, HA * NS)
        dec_diag = tiny(HA * NS, HA * NS)
        dec_inv = tiny(P, HA, NS)
        o_new = tiny(P, 4, NS)
        dec_m = tiny(HA * NS, 1)
        logits = part(attn_flat, ALLP, 1024, 3, NE)
        rest = part(attn_flat, ALLP, 1120, 3, NE)
        chosen = part(attn_flat, ALLP, 1216, 3, NE)
        top8 = part(attn_flat, ALLP, 1312, 3, 8)
        keys8 = part(attn_flat, ALLP, 1336, 3, 8)
        b_r = part(attn_flat, ALLP, 1360, NE)
        rounds_f = tiny(P, 2)
        rounds_i = sb("rounds_i", [1, 1], I32)
        row_t = attn_flat[:, 384:384 + T]

        landed = [sem(f"landed{s}") for s in range(SLOTS)]
        items_used = sem("items_used")
        keys_used = sem("keys_used")
        vector_full, vector_free = sem("vector_full"), sem("vector_free")
        scalar_full, scalar_free = sem("scalar_full"), sem("scalar_free")
        query_full, query_free = sem("query_full"), sem("query_free")
        vstep, astep, gstep = sem("vstep"), sem("astep"), sem("gstep")
        named = {}

        def sig(name):
            if name not in named:
                named[name] = sem("s_" + name)
            return named[name]

        v_index, a_index, q_index = {}, {}, {}
        freed = {}
        slot_count = [0] * SLOTS
        landing = {}
        for n, item in enumerate(ITEMS):
            s = n % SLOTS
            slot_count[s] += 16 * (PAGES if item[0] in "KV" else 1)
            landing[item] = (s, slot_count[s])

        def slot_ap(item):
            return ring[:, landing[item][0], :]

        def arrived(eng, item):
            eng.wait_ge(landed[landing[item][0]], landing[item][1])

        def gu_done(n, j, first):
            return n * 12 + (8 if j else 4 if first else 2)

        def down_done(n, j, last):
            return n * 12 + (10 if j == 0 else 12 if last else 16)

        def expert_landing(kind, s, e, edge):
            if kind == "gu":
                slot, value = (s, e + 1) if edge else (4 + s, e) if s < 2 else (s - 2, e + 1)
            else:
                slot, value = (4 + s, e + 1) if edge else (2 + s, e + 2)
            slot = EXPERT_SLOTS[slot]
            return slot, value * 16 + slot_count[slot]

        block = ctx.enter_context(nc.Block())

        @block.tensor
        def _(pe):
            def vector_bank():
                n = len(v_index)
                if n >= 3:
                    pe.wait_ge(vector_free, n - 2)
                return ps[:, 2 + n % 3, :]

            def vector_filled(ins, name):
                ins.then_inc(vector_full, 1)
                v_index[name] = len(v_index) + 1

            def scalar_bank():
                n = len(a_index)
                if n >= 2:
                    pe.wait_ge(scalar_free, n - 1)
                return ps[:, n % 2, :]

            def scalar_filled(ins, name):
                ins.then_inc(scalar_full, 1)
                a_index[name] = len(a_index) + 1

            def from_vector(name):
                pe.wait_ge(vector_free, v_index[name])

            def from_scalar(name):
                pe.wait_ge(scalar_free, a_index[name])

            used = [0]

            def release(ins, item):
                ins.then_inc(items_used, 1)
                used[0] += 1
                freed[item] = (items_used, used[0])

            def transpose(out, in_):
                n = in_.shape[0]
                return pe.transpose(out, in_, ident[0:n, 0:n])

            pe.wait_ge(sig("ones"), 1)
            pe.wait_ge(sig("ident"), 1)
            pe.wait_ge(sig("vec_rows"), 16 * len(VEC_ROWS))
            bank = vector_bank()
            vector_filled(transpose(bank[:, 0:N_VEC], vec_rows), "vectors")
            pe.wait_ge(sig("c_silu"), 1)
            bank = vector_bank()
            for k in range(KT):
                ins = transpose(bank[:, 9 * k:9 * k + 9], c_rows[:, k * P:(k + 1) * P])
            vector_filled(ins, "cT")
            pe.wait_ge(sig("x_tok"), 32)
            for k in range(KT):
                bank = vector_bank()
                for t, (t0, tn) in enumerate(TOK_TILES):
                    ins = transpose(bank[:, t0:t0 + tn], tok[0:tn, t, k * P:(k + 1) * P])
                vector_filled(ins, f"xT{k}")

            def modulate(first, bank, n_parts):
                for n in n_parts:
                    item = f"ada{first + n}"
                    arrived(pe, item)
                    w = slot_ap(item)[:, 0:4096].rearrange("p (k c) -> p k c", k=2)
                    for kk in range(2):
                        for m in range(16):
                            ins = pe.matmul(bank[:, 9 * m:9 * m + 9], w[:, kk, m * P:(m + 1) * P],
                                            cT[:, 2 * n + kk, :], start=(n == 0 and kk == 0 and m == 0),
                                            stop=(n == 3 and kk == 1), skip_group_check=True)
                    if n < 3:
                        release(ins, item)
                    else:
                        vector_filled(ins, f"mod{first // 4}")
                        freed[item] = (vector_full, len(v_index))

            from_vector("cT")
            modulate(0, vector_bank(), range(4))
            pe.wait_ge(sig("rstd_diag"), 1)
            bank = vector_bank()
            for t, (t0, tn) in enumerate(TOK_TILES):
                ins = pe.matmul(bank[:, t0:t0 + tn], ones[0:tn, :], rstd_diag[0:tn, t, 0:tn],
                                start=True, stop=True)
            vector_filled(ins, "rstd")

            def project(item, col, width, name, last=False, free=True):
                w = slot_ap(item)[:, 0:WIN[item][1] * KT].rearrange("p (k c) -> p k c", k=KT)
                c0 = col - WIN[item][0]
                to_vector = name == "fa"
                bank = vector_bank() if to_vector else scalar_bank()
                for k in range(KT):
                    ins = pe.matmul(bank[0:width, 0:T], w[:, k, c0:c0 + width], hT[:, k, :],
                                    start=(k == 0), stop=(k == KT - 1))
                if to_vector:
                    vector_filled(ins, name)
                else:
                    scalar_filled(ins, name)
                if last:
                    freed[item] = (scalar_full, len(a_index))

            def query_rows(b):
                if b >= 2:
                    pe.wait_ge(query_free, b - 1)
                ins = pe.matmul(ps[:, 5 + b % 2, :], ident[0:NS, b:b + 1].to_broadcast([NS, P]), q_rows,
                                start=True, stop=True)
                ins.then_inc(query_full, 1)

            pe.wait_ge(sig("hT"), 1)
            arrived(pe, "qa")
            for i in range(4):
                project("qa", QA + i * P, P, f"q{i}", last=(i == 3))
            arrived(pe, "ka")
            project("ka", KA, P, "k0")
            bank = vector_bank()
            from_scalar("q3")
            for i in range(4):
                ins = transpose(bank[0:NS, i * P:(i + 1) * P], qT[:, i, TP:T])
            vector_filled(ins, "q_rows")
            for i in range(1, 4):
                project("ka", KA + i * P, P, f"k{i}", last=(i == 3))
            from_vector("q_rows")
            query_rows(0)
            query_rows(1)
            arrived(pe, "va")
            for i in range(4):
                project("va", VA + i * P, P, f"v{i}", last=(i == 3))
            arrived(pe, "fqk")
            project("fqk", FA, HA, "fa")
            for name, src in (("k", kT), ("v", vT)):
                from_scalar(f"{name}3")
                for t, (t0, tn) in enumerate(TOK_TILES):
                    bank = vector_bank()
                    for i in range(4):
                        ins = transpose(bank[0:tn, i * P:(i + 1) * P], src[:, i, t0:t0 + tn])
                    vector_filled(ins, f"{name}_tok{t}")
            project("fqk", QB, P, "qb0")
            pe.wait_ge(sig("neg_cum"), 1)
            bank = vector_bank()
            for t, (t0, tn) in enumerate(TOK_TILES):
                transpose(bank[0:tn, t * HA:(t + 1) * HA], fT[:, t0:t0 + tn])
            for t in range(2):
                ins = transpose(bank[:, (3 + t) * HA:(4 + t) * HA], neg_cum[0:HA, t * P:(t + 1) * P])
            vector_filled(ins, "f_tok")
            pe.wait_ge(sig("qk_new"), 1)
            bank = vector_bank()
            pe.matmul(bank[:, 0:HA * NS], ones[:, :], qk_new.rearrange("p a b -> p (a b)"), start=True, stop=True)
            ins = pe.matmul(bank[:, HA * NS:2 * HA * NS], ones[0:NS, :], f_diag.rearrange("p a b -> p (a b)"),
                            start=True, stop=True)
            vector_filled(ins, "new")

            def head_scores(h):
                i, half = h // 2, slice(64 * (h % 2), 64 * (h % 2) + 64)
                bank = vector_bank()
                for t in range(2):
                    c0, n = (0, P) if t == 0 else (P, 2 * P)
                    pe.matmul(bank[:, c0:c0 + n], qT[half, i, t * P:(t + 1) * P], kT[half, i, 0:n],
                              start=True, stop=False)
                    row = 64 * (h % 2) + h
                    ins = pe.matmul(bank[:, c0:c0 + n], ident[half, row:row + 1].to_broadcast([64, P]),
                                    neg_cum[half, 0:n], start=False, stop=True)
                vector_filled(ins, f"scores{h}")

            def head_turn(h):
                pe.wait_ge(sig("probs"), h + 1)
                bank = scalar_bank()
                for j in range(3):
                    ins = transpose(bank[:, j * P:(j + 1) * P], attn[:, h % 2, j * P:(j + 1) * P])
                scalar_filled(ins, f"turned{h}")

            pv_bank = [None]

            def head_values(h):
                from_scalar(f"turned{h}")
                if h % 2 == 0:
                    pv_bank[0] = vector_bank()
                half = slice(64 * (h % 2), 64 * (h % 2) + 64)
                out = pv_bank[0][half, :]
                pT = attn[:, 2 + h % 2, :]
                v = v_tok[:, :, h * DH:(h + 1) * DH]
                pe.matmul(out[:, 0:P], v[:, 0, :], pT[:, 0:P], start=True, stop=True)
                pe.matmul(out[:, P:2 * P], v[:, 0, :], pT[:, P:2 * P], start=True, stop=False)
                ins = pe.matmul(out[:, P:2 * P], v[:, 1, :], pT[:, 2 * P:3 * P], start=False, stop=True)
                if h % 2 == 1:
                    vector_filled(ins, f"o{h // 2}")
                else:
                    ins.then_inc(sig("pv_even"), 1)

            from_vector("v_tok1")
            tiles = ([("fqk", QB + P, P, "qb1"), ("fqk", KB, P, "kb0"), ("fqk", KB + P, P, "kb1")]
                     + [("vb", VB + i * P, P, f"vb{i}") for i in range(4)]
                     + [("rb", RB + i * P, P, f"rb{i}") for i in range(4)] + [("rb", ALR, 16, "alr")])
            for s in range(len(tiles)):
                item, col, width, name = tiles[s]
                if s == 0 or tiles[s - 1][0] != item:
                    arrived(pe, item)
                project(item, col, width, name, last=(s + 1 == len(tiles) or tiles[s + 1][0] != item))
                if s < HA:
                    head_scores(s)
                if 1 <= s <= HA:
                    head_turn(s - 1)
                if s % 2 == 1 and 3 <= s < HA + 3:
                    head_values(s - 3)
                    head_values(s - 2)
                if s % 2 == 0 and 2 + s // 2 < NS:
                    query_rows(2 + s // 2)

            from_scalar("alr")
            pe.wait_ge(sig("small_loads"), 32)
            for i in range(2):
                bank = vector_bank()
                vector_filled(pe.matmul(bank[:, 0:T], w_alpha_sb[:, i * P:(i + 1) * P], alrT[:, :],
                                        start=True, stop=True), f"alpha{i}")
            for c in range(NCH):
                bank = scalar_bank()
                for h in range(HB):
                    ins = transpose(bank[0:CH, h * DV:(h + 1) * DV], vbT[:, h, c * CH:(c + 1) * CH])
                scalar_filled(ins, f"vb_tok{c}")
            bank = vector_bank()
            for h in range(HB):
                ins = transpose(bank[0:NS, h * DV:(h + 1) * DV], vbT[:, h, TP:T])
            vector_filled(ins, "vb_rows")
            pe.wait_ge(sig("lf_rows"), 16)
            bank = vector_bank()
            for h in range(HA):
                ins = transpose(bank[:, h * 64:(h + 1) * 64], lf_rows[:, h:h + HA * (PAGE - 1) + 1:HA])
            vector_filled(ins, "past_lf")
            from_vector("past_lf")
            pe.wait_ge(sig("tri"), 5)
            bank = vector_bank()
            vector_filled(pe.matmul(bank[:, :], ones[:, :], past_lf.rearrange("p a b -> p (a b)"),
                                    start=True, stop=True), "page_sums")
            bank = vector_bank()
            vector_filled(pe.matmul(bank[:, :], after[:, :], past_lf.rearrange("p a b -> p (a b)"),
                                    start=True, stop=True), "in_page_suffix")
            pe.wait_ge(sig("qg_kg"), 2)
            for i in range(2):
                for f in range(2):
                    half = slice(64 * f, 64 * f + 64)
                    bank = vector_bank()
                    for c in range(NCH):
                        ins = pe.matmul(bank[0:CH, c * CH:(c + 1) * CH], e_k[half, i * NCH + c, :],
                                        e_q[half, i * NCH + c, :], start=True, stop=True)
                    vector_filled(ins, f"A{i}{f}")
            pe.wait_ge(sig("kd"), 1)
            for i in range(2):
                bank = scalar_bank()
                for c in range(NCH):
                    ins = transpose(bank[0:CH, c * P:(c + 1) * P], al_d[:, i * NCH + c, :])
                scalar_filled(ins, f"kd_tok{i}")
            from_scalar("kd_tok1")
            for i in range(2):
                for c2 in range(2):
                    bank = vector_bank()
                    for c in (2 * c2, 2 * c2 + 1):
                        ins = pe.matmul(bank[:, (c % 2) * 256:(c % 2) * 256 + 256], kd_tok[:, i, c, :],
                                        vb_tok[:, c, i * 256:(i + 1) * 256], start=True, stop=True)
                    vector_filled(ins, f"kv{i}{c2}")
            pe.wait_ge(sig("qe"), 1)
            from_vector("kv11")
            for h in range(HB):
                i, f = h // 2, h % 2
                bank = vector_bank()
                for c in range(NCH):
                    ins = pe.matmul(bank[:, c * CH:(c + 1) * CH], vb_tok[:, c, h * DV:(h + 1) * DV],
                                    A_T[:, i, f, c * CH:(c + 1) * CH], start=True, stop=(c == 0))
                    if c:
                        ins = pe.matmul(bank[:, c * CH:(c + 1) * CH], gla_S[:, c - 1, i, :],
                                        qe[:, f, i * NCH + c, :], start=False, stop=True)
                vector_filled(ins, f"ob{h}")

            from_vector("vb_rows")
            for b in range(NS):
                bank = vector_bank()
                vector_filled(pe.matmul(bank[:, :], ident[0:NS, b:b + 1].to_broadcast([NS, P]), vb_rows,
                                        start=True, stop=True), f"v_row{b}")
            from_vector("v_row7")
            state = slot_ap("state")[:, 0:NS * 2 * DV].rearrange("p (b i v) -> p b i v", b=NS, i=2)
            bank = vector_bank()
            out = bank[:, 0:64].rearrange("p (i f b) -> p i f b", i=2, f=2, b=16)[:, :, :, 0:NS]
            for b in range(NS):
                for i in range(2):
                    ins = pe.matmul(out[:, i, :, b], state[:, b, i, :], qb_new[:, i, b, :],
                                    start=True, stop=True)
            vector_filled(ins, "ob_new")
            freed["state"] = (vector_full, len(v_index))
            pe.wait_ge(sig("ob_sq"), 1)
            for h in range(HB):
                bank = vector_bank()
                vector_filled(pe.matmul(bank[:, 0:T], ones[:, :], ob_sq[:, h, :], start=True, stop=True),
                              f"ob_ss{h}")

            pe.wait_ge(sig("dec_max"), 1)
            bank = vector_bank()
            vector_filled(transpose(bank[0:64, 0:P], dec_max), "dec_maxT")
            pe.wait_ge(sig("dec_diag"), 1)
            bank = vector_bank()
            vector_filled(pe.matmul(bank[:, 0:64], ones[0:64, :], dec_diag, start=True, stop=True), "dec_top")
            pe.wait_ge(sig("dec_probs"), 1)
            bank = vector_bank()
            vector_filled(pe.matmul(bank[:, :], ones[:, :], dec_scores[:, :, :].rearrange("p a b -> p (a b)"),
                                    start=True, stop=True), "dec_sums")
            out = ps[:, 7, 0:64].rearrange("p (i b f) -> p i b f", i=4, b=NS)
            for b in range(NS):
                arrived(pe, f"V{b}")
                v = slot_ap(f"V{b}")[:, 0:PAGES * WA].rearrange("p (j c) -> p j c", j=PAGES)
                for i in range(4):
                    for j in range(PAGES):
                        ins = pe.matmul(out[:, i, b, :], v[:, j, i * P:(i + 1) * P],
                                        dec_scores[:, 2 * i * NS + b:(2 * i + 1) * NS + b + 1:NS, j],
                                        start=(j == 0), stop=(j == PAGES - 1))
                release(ins, f"V{b}")

            pe.wait_ge(sig("gla_done"), 1)
            for step, item in enumerate(["ga0", "ga1", "gb0", "gb1"]):
                arrived(pe, item)
                for m in range(4):
                    project(item, WIN[item][0] + m * P, P, f"{item}_{m}", last=(m == 3))
                if step % 2 == 0:
                    mod_bank = vector_bank()
                modulate(4 + 4 * (step // 2), mod_bank, range(2 * (step % 2), 2 * (step % 2) + 2))
            arrived(pe, "wb0")
            arrived(pe, "wb1")
            pe.wait_ge(sig("oT"), 1)
            wb = [slot_ap(f"wb{n}")[:, 0:4096].rearrange("p (k c) -> p k c", k=4) for n in range(2)]
            for m in range(KT):
                for n, src in enumerate((oT[:, :, :], obT)):
                    bank = vector_bank()
                    for k in range(4):
                        ins = pe.matmul(bank[:, 0:T], wb[n][:, k, m * P:(m + 1) * P], src[:, k, :],
                                        start=(k == 0), stop=(k == 3))
                    vector_filled(ins, f"y{n}_{m}")
            freed["wb0"] = freed["wb1"] = (vector_full, len(v_index))
            pe.wait_ge(sig("mixed"), 1)
            arrived(pe, "wo0")
            arrived(pe, "wo1")
            wo = [slot_ap(f"wo{n}")[:, 0:4096].rearrange("p (k c) -> p k c", k=4) for n in range(2)]
            for m in range(KT):
                bank = vector_bank()
                for k in range(KT):
                    ins = pe.matmul(bank[:, 0:T], wo[k // 4][:, k % 4, m * P:(m + 1) * P], hT[:, k, :],
                                    start=(k == 0), stop=(k == KT - 1))
                vector_filled(ins, f"out{m}")
            freed["wo0"] = freed["wo1"] = (vector_full, len(v_index))
            def sum_squares(name, ready):
                pe.wait_ge(sig(ready), 1)
                bank = vector_bank()
                for k in range(KT):
                    ins = pe.matmul(bank[:, 0:T], ones[:, :], sq_zone[:, k, :], start=(k == 0), stop=(k == KT - 1))
                vector_filled(ins, name)

            sum_squares("x1_ss", "x1_sq")
            pe.wait_ge(sig("h2T"), 1)
            pe.wait_ge(sig("w_r"), 16)
            bank = vector_bank()
            for t, (t0, tn) in enumerate(TOK_TILES):
                for k in range(KT):
                    ins = pe.matmul(bank[0:tn, t * NE:(t + 1) * NE], hT[:, k, t0:t0 + tn], w_r[:, k, :],
                                    start=(k == 0), stop=(k == KT - 1))
            vector_filled(ins, "logits")
            for t, (t0, tn) in enumerate(TOK_TILES):
                for g in range(2):
                    bank = scalar_bank()
                    for k in range(4):
                        ins = transpose(bank[0:tn, k * P:(k + 1) * P], hT[:, 4 * g + k, t0:t0 + tn])
                    scalar_filled(ins, f"h2_tok{t}{g}")
            pe.wait_ge(sig("chosen"), 3)
            bank = vector_bank()
            for t, (t0, tn) in enumerate(TOK_TILES):
                for u in range(t):
                    pe.matmul(bank[0:tn, t * NE:(t + 1) * NE], ones[:, 0:tn], chosen[:, u, :],
                              start=(u == 0), stop=False)
                pe.matmul(bank[0:tn, t * NE:(t + 1) * NE], before[0:tn, 0:tn], chosen[0:tn, t, :],
                          start=(t == 0), stop=True)
            for t, (t0, tn) in enumerate(TOK_TILES):
                ins = pe.matmul(bank[:, 3 * NE:4 * NE], ones[0:tn, :], chosen[0:tn, t, :],
                                start=(t == 0), stop=(t == 2))
            vector_filled(ins, "places")
            pe.wait_ge(sig("gates"), 3)
            bank = vector_bank()
            for t, (t0, tn) in enumerate(TOK_TILES):
                ins = transpose(bank[0:NE, t0:t0 + tn], gates[0:tn, t, :])
            vector_filled(ins, "gatesT")
            from_vector("gatesT")
            pe.wait_ge(sig("b_d"), 16)
            for m in range(KT):
                bank = vector_bank()
                vector_filled(pe.matmul(bank[:, 0:T], b_d_sb[:, m * P:(m + 1) * P], gatesT, start=True, stop=True),
                              f"bias{m}")

            def gather(n):
                pe.wait_ge(sig("pick_ready"), n + 1)
                for k in range(KT):
                    out = ps[:, 6 + k // 4, (k % 4) * P:(k % 4 + 1) * P]
                    for t, (t0, tn) in enumerate(TOK_TILES):
                        ins = pe.matmul(out, tok[0:tn, t, k * P:(k + 1) * P], pick[0:tn, t, :],
                                        start=(t == 0), stop=(t == 2))
                    if k % 4 == 3:
                        ins.then_inc(sig("gathered"), 1)

            def expert_slot(kind, s, e, edge):
                slot, value = expert_landing(kind, s, e, edge)
                pe.wait_ge(landed[slot], value)
                return ring[:, slot, :]

            def gate_up(n, j, edge, first, between):
                e = 2 * n + j
                if not first:
                    pe.wait_ge(sig("up_clipped"), e - 1)
                banks = ps[:, 2 * j:2 * j + 2, :]
                for c in range(2):
                    for half in range(2):
                        pe.matmul(banks[64 * half:64 * half + CAP, c, :], expert_row[:, j, :],
                                  b_gu_rows[:, half * FF + c * 512:half * FF + (c + 1) * 512],
                                  start=True, stop=False, skip_group_check=True)
                for s in range(4):
                    w = expert_slot("gu", s, e, edge)[:, 0:4096].rearrange("p (k c) -> p k c", k=2)
                    for kk in range(2):
                        k = 2 * s + kk
                        if j == 0 and k % 4 == 0:
                            pe.wait_ge(sig("xg_ready"), 2 * n + 1 + k // 4)
                        for c in range(2):
                            for half in range(2):
                                ins = pe.matmul(banks[64 * half:64 * half + CAP, c, :],
                                                xg[:, k, j * CAP:(j + 1) * CAP],
                                                w[:, kk, half * FF + c * 512:half * FF + (c + 1) * 512],
                                                start=False, stop=(k == KT - 1), skip_group_check=True)
                        if kk == 1:
                            ins.then_inc(sig("slots_used"), 1)
                        else:
                            between(k)

            def turn_hidden(n, j, first):
                pe.wait_ge(sig("hid_ready"), 2 * n + j + 1)
                if not first:
                    pe.wait_ge(sig("turn_read"), 3 * n + j)
                for k in range(KT):
                    ins = pe.matmul(ps[:, 4, k * CAP:(k + 1) * CAP], hid[:, k * P:(k + 1) * P],
                                    ident[0:CAP, 0:CAP], start=True, stop=True)
                ins.then_inc(sig("turned"), 1)

            def turn_put(n):
                pe.wait_ge(sig("put_ready"), n + 1)
                pe.wait_ge(sig("turn_read"), 3 * n + 2)
                for t, (t0, tn) in enumerate(TOK_TILES):
                    ins = transpose(ps[:, 4, t0:t0 + tn], put[0:tn, t, :])
                ins.then_inc(sig("turned"), 1)

            def down(n, j, edge, first):
                e = 2 * n + j
                pe.wait_ge(sig("turn_read"), 3 * n + 1 + j)
                if not first:
                    pe.wait_ge(sig("ye_ready"), e)
                for s in range(2):
                    w = expert_slot("dn", s, e, edge)[:, 0:4096].rearrange("p (k c) -> p k c", k=4)
                    for kk in range(4):
                        k = 4 * s + kk
                        for half in range(2):
                            ins = pe.matmul(ps[64 * half:64 * half + CAP, 5, :], hidT[:, k, :],
                                            w[:, kk, half * 512:(half + 1) * 512],
                                            start=(k == 0), stop=(k == KT - 1), skip_group_check=True)
                    ins.then_inc(sig("slots_used"), 1)

            def combine(n, ms):
                for m in ms:
                    if m == 0:
                        pe.wait_ge(sig("ye_ready"), 2 * n + 2)
                    if m >= 2:
                        pe.wait_ge(sig("added"), n * KT + (m - 1))
                    pe.matmul(ps[:, 6 + m % 2, 0:T], ye_tok[:, m * P:(m + 1) * P], putT,
                              start=True, stop=True).then_inc(sig("combined"), 1)

            def pair(n, first, last, cold):
                def beside_b(k):
                    if not first:
                        combine(n - 1, (k, k + 1))
                    if k == 4:
                        turn_hidden(n, 0, cold)

                def beside_next_a(k):
                    if k == 2:
                        turn_hidden(n, 1, False)
                    if k == 6:
                        turn_put(n)

                gate_up(n, 1, False, cold, beside_b)
                if not last:
                    if not first:
                        pe.wait_ge(sig("added"), n * KT)
                    gather(n + 1)
                down(n, 0, False, cold)
                if not last:
                    gate_up(n + 1, 0, False, False, beside_next_a)
                else:
                    turn_hidden(n, 1, False)
                    turn_put(n)
                down(n, 1, last, False)

            def one_round(rnd):
                n = rnd * PAIRS
                cold = isinstance(rnd, int)
                if not cold:
                    pe.wait_ge(sig("added"), n * KT)
                gather(n)
                gate_up(n, 0, True, cold, lambda k: None)
                pair(n, True, False, cold)
                with pe.Fori(1, PAIRS - 1) as p:
                    pair(n + p, False, False, False)
                pair(n + (PAIRS - 1), False, True, False)
                combine(n + (PAIRS - 1), range(KT))

            pe.wait_ge(sig("b_gu_rows"), 16)
            pe.wait_ge(vector_free, len(v_index))
            pe.wait_ge(scalar_free, len(a_index))
            one_round(0)
            pe.wait_ge(sig("rounds"), 1)
            rounds = pe.value_load(rounds_i[0:1, 0:1], min_val=1, max_val=MAX_ROUNDS)
            with pe.If(rounds > 1):
                with pe.Fori(1, rounds) as rnd:
                    one_round(rnd)

            sum_squares("x2_ss", "x2_sq")
            pe.wait_ge(sig("yT"), 1)
            for t, (t0, tn) in enumerate(TOK_TILES):
                for g in range(2):
                    bank = scalar_bank()
                    for k in range(4):
                        ins = transpose(bank[0:tn, k * P:(k + 1) * P], hT[:, 4 * g + k, t0:t0 + tn])
                    scalar_filled(ins, f"y_tok{t}{g}")

        @block.scalar
        def _(act):
            def dma(out, in_, name):
                act.dma_start(out, in_).then_inc(sig(name), 16)

            def row(vec, n):
                return vec[0].rearrange("(r p) -> r p", p=P)[0:n, :]

            dma(c_rows[0:1, :], c_prompt, "c_rows")
            dma(c_rows[1:9, :], c_sample, "c_rows")
            dma(tok[:, 0:2, :], x_prompt[0].rearrange("(t p) d -> p t d", p=P), "x_tok")
            dma(tok[0:NS, 2, :], x_sample.rearrange("b s d -> (b s) d"), "x_tok")
            vectors = {"b_ada": b_ada, "g_mix": g_mix, "g_ffn": g_ffn, "g_gla": g_gla, "b_alpha": b_alpha}
            for name, (r0, n) in VEC_ROWS.items():
                src = row(vectors[name], n) if name != "g_final" else g_final.rearrange("(r p) -> r p", p=P)
                dma(vec_rows[r0:r0 + n, :], src, "vec_rows")
            dma(pages_row[:, :], page_table.rearrange("b (a j) -> a (b j)", a=1), "pages")
            dma(pages_col[:, :], page_table.rearrange("b (j a) -> (b j) a", a=1), "pages")
            dma(w_alpha_sb[:, :], w_alpha[0], "small_loads")
            dma(b_f_col[:, :], b_f[0].rearrange("(h a) -> h a", a=1), "small_loads")

            def take(name):
                act.wait_ge(scalar_full, a_index[name])
                return ps[:, (a_index[name] - 1) % 2, :]

            def copy_out(dst, name, rows=P, cols=T, func=ACT.Copy, scale=1.0):
                bank = take(name)
                src = bank[0:rows, 0:cols]
                if len(dst.shape) == 3:
                    src = src.rearrange("p (a b) -> p a b", b=dst.shape[2])
                nc.scalar.activation(dst, src, func, scale=scale).then_inc(scalar_free, 1)

            def log1p_exp(x, ready, done):
                act.wait_ge(sig(ready), 1)
                nc.scalar.activation(x, x, ACT.Exp).then_inc(sig(ready), 1)
                act.wait_ge(sig(ready), 2)
                nc.scalar.activation(x, x, ACT.Ln, bias=1.0).then_inc(sig(done), 1)

            act.wait_ge(sig("c_rows"), 32)
            nc.scalar.activation(c_rows, c_rows, ACT.Silu).then_inc(sig("c_silu"), 1)
            act.wait_ge(sig("x_tok"), 32)
            act.wait_ge(sig("ssq_ones"), 1)
            for t, (t0, tn) in enumerate(TOK_TILES):
                if t:
                    act.wait_ge(sig("ssq"), t)
                nc.scalar.activation(junk[0:tn, :], tok[0:tn, t, :], ACT.Square,
                                     accum_out=ssq[0:tn, t:t + 1]).then_inc(sig("ssq"), 1)
            act.wait_ge(sig("x_var"), 1)
            nc.scalar.activation(rstd, rstd, ACT.Sqrt).then_inc(sig("x_rms"), 1)
            for i in range(4):
                copy_out(qT[:, i, :], f"q{i}", scale=SCALE)
            for name, dst in (("k", kT), ("v", vT)):
                for i in range(4):
                    copy_out(dst[:, i, :], f"{name}{i}")
            log1p_exp(f_nabs, "f_nabs", "f_log")

            def tile_out(name):
                i = int(name[-1]) if name != "alr" else 0
                if name == "alr":
                    copy_out(alrT, name, rows=16)
                elif name.startswith("qb"):
                    copy_out(qbT[:, i, :], name, scale=DK ** -0.5)
                elif name.startswith("kb"):
                    copy_out(kbT[:, i, :], name)
                elif name.startswith("vb"):
                    copy_out(vbT[:, i, :], name)
                else:
                    copy_out(rbT[:, i, :], name, func=ACT.Silu)

            def head_exp(h):
                act.wait_ge(sig("neg_max"), h + 1)
                sc = attn[:, h % 2, :]
                nc.scalar.activation(sc[:, 0:P], sc[:, 0:P], ACT.Exp, bias=row_max[:, 2 * h:2 * h + 1],
                                     accum_out=row_sum[:, 2 * h:2 * h + 1])
                nc.scalar.activation(sc[:, P:3 * P], sc[:, P:3 * P], ACT.Exp,
                                     bias=row_max[:, 2 * h + 1:2 * h + 2],
                                     accum_out=row_sum[:, 2 * h + 1:2 * h + 2]).then_inc(sig("exps"), 1)

            def head_turned(h):
                if h >= 2 and h % 2 == 0:
                    act.wait_ge(sig("pv_even"), h // 2)
                if h >= 2 and h % 2 == 1:
                    act.wait_ge(vector_full, v_index[f"o{h // 2 - 1}"])
                copy_out(attn[:, 2 + h % 2, :], f"turned{h}", cols=3 * P)

            tile_out("qb0")
            names = ["qb1", "kb0", "kb1"] + [f"vb{i}" for i in range(4)] + [f"rb{i}" for i in range(4)] + ["alr"]
            for s, name in enumerate(names):
                tile_out(name)
                if 1 <= s <= HA:
                    head_turned(s - 1)
                if s < HA:
                    head_exp(s)
            for c in range(NCH):
                copy_out(vb_tok[:, c, :], f"vb_tok{c}", rows=CH, cols=512)
            log1p_exp(al_nabs, "al_nabs", "al_log")
            act.wait_ge(sig("al_d"), 1)
            d = al_d.rearrange("p a b -> p (a b)")
            nc.scalar.activation(e_q.rearrange("p a b -> p (a b)"), d, ACT.Exp).then_inc(sig("al_exp"), 1)
            nc.scalar.activation(e_k.rearrange("p a b -> p (a b)"), d, ACT.Exp, scale=-1.0)\
                .then_inc(sig("al_exp"), 1)
            nc.scalar.activation(e_b.rearrange("p a b -> p (a b)"), al_b.rearrange("p a b -> p (a b)"),
                                 ACT.Exp).then_inc(sig("al_exp"), 1)
            act.wait_ge(sig("la_new"), 1)
            nc.scalar.activation(la_new, la_new, ACT.Exp).then_inc(sig("a_new"), 1)
            act.wait_ge(sig("al_rest"), 1)
            nc.scalar.activation(d, d, ACT.Exp).then_inc(sig("rest_exp"), 1)
            for i in range(2):
                copy_out(kd_tok[:, i, :, :].rearrange("p c k -> p (c k)"), f"kd_tok{i}", rows=CH, cols=512)
            act.wait_ge(vector_free, v_index[f"ob_ss{HB - 1}"])
            nc.scalar.activation(ob_rs, ob_rs, ACT.Sqrt).then_inc(sig("ob_rms"), 1)
            act.wait_ge(sig("dec_shift"), 1)
            nc.scalar.activation(dec_scores[:, :, :], dec_scores[:, :, :], ACT.Exp)
            nc.scalar.activation(s_new, s_new, ACT.Exp).then_inc(sig("dec_probs"), 1)
            for item in ("ga0", "ga1", "gb0", "gb1"):
                dst = gaT if item[1] == "a" else gbT
                for m in range(4):
                    copy_out(dst[:, 4 * int(item[2]) + m, :], f"{item}_{m}", func=ACT.Sigmoid)

            def squares_and_root(x_ready, sq_ready, sums, rms_ready):
                act.wait_ge(sig(x_ready), 1)
                nc.scalar.activation(sq_zone, xT[:, :, :], ACT.Square).then_inc(sig(sq_ready), 1)
                act.wait_ge(vector_free, v_index[sums])
                nc.scalar.activation(row_t, row_t, ACT.Sqrt).then_inc(sig(rms_ready), 1)

            squares_and_root("x1", "x1_sq", "x1_ss", "x1_rms")
            for t, (t0, tn) in enumerate(TOK_TILES):
                for g in range(2):
                    copy_out(tok[0:tn, t, g * 512:(g + 1) * 512], f"h2_tok{t}{g}", rows=tn, cols=512)
            for t, (t0, tn) in enumerate(TOK_TILES):
                act.wait_ge(sig("top_neg"), t + 1)
                nc.scalar.activation(logits[0:tn, t, :], logits[0:tn, t, :], ACT.Exp,
                                     bias=keys8[0:tn, t, 7:8]).then_inc(sig("top_exp"), 1)

            def take_gathered(n):
                for g in range(2):
                    act.wait_ge(sig("gathered"), 2 * n + g + 1)
                    nc.scalar.activation(xg[:, 4 * g:4 * g + 4, :].rearrange("p a b -> p (a b)"),
                                         ps[:, 6 + g, :], ACT.Copy).then_inc(sig("xg_ready"), 1)

            def sigmoid(n, j):
                act.wait_ge(sig("gate_ready"), 2 * n + j + 1)
                nc.scalar.activation(sig_v, gate_v, ACT.Sigmoid, scale=ALPHA).then_inc(sig("sig_ready"), 1)

            def take_hidden(n, j):
                act.wait_ge(sig("turned"), 3 * n + 1 + j)
                nc.scalar.activation(hidT, ps[:, 4, :].rearrange("p (k c) -> p k c", c=CAP), ACT.Copy)\
                    .then_inc(sig("turn_read"), 1)

            def take_put(n):
                act.wait_ge(sig("turned"), 3 * n + 3)
                nc.scalar.activation(putT, ps[:, 4, 0:T], ACT.Copy).then_inc(sig("turn_read"), 1)

            def take_output(n, j, last):
                act.wait_ge(sig("slots_used"), down_done(n, j, last))
                for half in range(2):
                    ins = nc.scalar.activation(ye_tok[64 * j:64 * j + CAP, half * 512:(half + 1) * 512],
                                               ps[64 * half:64 * half + CAP, 5, :], ACT.Copy)
                ins.then_inc(sig("ye_ready"), 1)

            def pair(n, first, last):
                take_hidden(n, 0)
                sigmoid(n, 1)
                if not last:
                    take_gathered(n + 1)
                if not first:
                    act.wait_ge(sig("combined"), n * KT)
                take_output(n, 0, False)
                take_hidden(n, 1)
                take_put(n)
                if not last:
                    sigmoid(n + 1, 0)
                take_output(n, 1, last)

            def one_round(rnd):
                n = rnd * PAIRS
                if not isinstance(rnd, int):
                    act.wait_ge(sig("combined"), n * KT)
                take_gathered(n)
                sigmoid(n, 0)
                pair(n, True, False)
                with act.Fori(1, PAIRS - 1) as p:
                    pair(n + p, False, False)
                pair(n + (PAIRS - 1), False, True)

            one_round(0)
            act.wait_ge(sig("rounds"), 1)
            rounds = act.value_load(rounds_i[0:1, 0:1], min_val=1, max_val=MAX_ROUNDS)
            with act.If(rounds > 1):
                with act.Fori(1, rounds) as rnd:
                    one_round(rnd)
            squares_and_root("x2", "x2_sq", "x2_ss", "x2_rms")
            for t, (t0, tn) in enumerate(TOK_TILES):
                for g in range(2):
                    copy_out(tok[0:tn, t, g * 512:(g + 1) * 512], f"y_tok{t}{g}", rows=tn, cols=512)
            act.wait_ge(scalar_free, len(a_index))
            act.dma_start(y_prompt[0].rearrange("(t p) d -> p t d", p=P), tok[:, 0:2, :]).then_inc(sig("stored"), 16)
            act.dma_start(y_sample.rearrange("b s d -> (b s) d"), tok[0:NS, 2, :]).then_inc(sig("stored"), 16)
            act.wait_ge(sig("stored"), 32)

        @block.vector
        def _(dve):
            steps = [0]

            def chain(ins):
                steps[0] += 1
                ins.then_inc(vstep, 1)
                dve.wait_ge(vstep, steps[0])

            def take(name):
                dve.wait_ge(vector_full, v_index[name])
                return ps[:, 2 + (v_index[name] - 1) % 3, :]

            def give(ins, name, then_read=False):
                ins.then_inc(vector_free, 1)
                if then_read:
                    dve.wait_ge(vector_free, v_index[name])

            V = nc.vector
            vec = {name: vecT[:, r0:r0 + n] for name, (r0, n) in VEC_ROWS.items()}

            def across(ap, n):
                return ap.unsqueeze(2).to_broadcast([ap.shape[0], ap.shape[1], n])

            V.memset(ssq, 1.0).then_inc(sig("ssq_ones"), 1)
            V.memset(qk_new, 0.0)
            V.memset(qb_new, 0.0)
            V.memset(vecT[:, :], 0.0)
            chain(V.memset(neg_cum[:, :], 0.0))
            give(V.tensor_copy(vecT[:, :], take("vectors")[:, 0:N_VEC]), "vectors")
            give(V.tensor_copy(cT[:, :, :], take("cT")[:, 0:9 * KT].rearrange("p (k c) -> p k c", c=9)), "cT")
            for k in range(KT):
                give(V.tensor_copy(xT[:, k, :], take(f"xT{k}")[:, 0:T]), f"xT{k}")
            dve.wait_ge(sig("ssq"), 3)
            V.tensor_scalar(rstd, ssq, 1.0 / D, EPS, ALU.mult, ALU.add).then_inc(sig("x_var"), 1)
            dve.wait_ge(sig("x_rms"), 1)
            chain(V.reciprocal(rstd, rstd))
            dve.wait_ge(sig("ident"), 1)
            for t in range(3):
                ins = V.tensor_scalar(rstd_diag[:, t, :], ident[:, :], rstd[:, t:t + 1], None, ALU.mult)
            ins.then_inc(sig("rstd_diag"), 1)

            def modulation(n):
                bank = take(f"mod{n}")
                give(V.tensor_tensor(modT[:, 16 * n:16 * n + 16, :],
                                     bank[:, 0:144].rearrange("p (m c) -> p m c", c=9),
                                     across(vec["b_ada"][:, 16 * n:16 * n + 16], 9), ALU.add),
                     f"mod{n}", then_read=True)

            def normed(gain, shift, g, scale):
                V.scalar_tensor_tensor(out=gain[:, :, :], in0=modT[:, scale:scale + KT, :], scalar=1.0,
                                       in1=across(vec[g], 9), op0=ALU.add, op1=ALU.mult)
                chain(V.tensor_tensor(hT[:, :, :], xT[:, :, :], row_t.unsqueeze(1).to_broadcast([P, KT, T]),
                                      ALU.mult))
                for k in range(KT):
                    V.tensor_scalar(hT[:, k, 0:TP], hT[:, k, 0:TP], gain[:, k, 0:1],
                                    modT[:, shift + k, 0:1], ALU.mult, ALU.add)
                chain(V.tensor_tensor(hT[:, :, TP:T], hT[:, :, TP:T], gain[:, :, 1:9], ALU.mult))
                return V.tensor_tensor(hT[:, :, TP:T], hT[:, :, TP:T], modT[:, shift:shift + KT, 1:9], ALU.add)

            modulation(0)
            give(V.tensor_copy(row_t, take("rstd")[:, 0:T]), "rstd", then_read=True)
            normed(gain1, 0, "g_mix", KT).then_inc(sig("hT"), 1)

            def keys_half(b, part_no):
                if part_no == 0:
                    arrived(dve, f"K{b}")
                    dve.wait_ge(query_full, b + 1)
                n = PAGES // 2
                kc = slot_ap(f"K{b}")[:, part_no * n * WA:(part_no + 1) * n * WA]\
                    .rearrange("p (j c) -> p j c", c=WA)
                ins = V.tensor_tensor(kc, kc, ps[:, 5 + b % 2, :].unsqueeze(1).to_broadcast([P, n, WA]), ALU.mult)
                if part_no == 1:
                    ins.then_inc(query_free, 1)
                    dve.wait_ge(query_free, b + 1)
                else:
                    chain(ins)
                V.tensor_reduce(dec_scores[:, b:HA * NS:NS, part_no * n:(part_no + 1) * n]
                                .rearrange("p h j -> p j h"),
                                kc.rearrange("p j (h d) -> p j h d", d=DH), AX_X, ALU.add)\
                    .then_inc(keys_used, 1)

            give(V.tensor_copy(q_rows, take("q_rows")[0:NS, :]), "q_rows")
            dve.wait_ge(scalar_free, a_index["k3"])
            qk = qk_new.rearrange("p (i f) b -> p i f b", f=2)
            for f in range(2):
                half = slice(64 * f, 64 * f + 64)
                ins = V.tensor_tensor(qk[half, :, f, :], qT[half, :, TP:T], kT[half, :, TP:T], ALU.mult)
            ins.then_inc(sig("qk_new"), 1)
            for b in range(2):
                for part_no in range(2):
                    keys_half(b, part_no)
            dve.wait_ge(sig("small_loads"), 32)
            give(V.tensor_scalar(fT, take("fa")[0:HA, 0:T], b_f_col[:, 0:1], None, ALU.add), "fa",
                 then_read=True)
            V.scalar_tensor_tensor(out=f_nabs, in0=fT, scalar=-1.0, in1=fT, op0=ALU.mult, op1=ALU.min)\
                .then_inc(sig("f_nabs"), 1)
            V.tensor_scalar(fT, fT, 0.0, None, ALU.min)
            for name, dst in (("k", k_tok), ("v", v_tok)):
                for t, (t0, tn) in enumerate(TOK_TILES):
                    out = dst[:, t, :] if t < 2 else k_new_rows if name == "k" else v_new_rows
                    give(V.tensor_copy(out, take(f"{name}_tok{t}")[0:tn, :]), f"{name}_tok{t}")
            dve.wait_ge(sig("f_log"), 1)
            chain(V.tensor_tensor(fT, fT, f_nabs, ALU.subtract))
            chain(V.tensor_tensor_scan(neg_cum[0:HA, 0:TP], ones[0:HA, 0:1].to_broadcast([HA, TP]), fT[:, 0:TP],
                                       0.0, ALU.mult, ALU.subtract))
            V.tensor_copy(neg_cum[64:64 + HA, 0:TP], neg_cum[0:HA, 0:TP])
            V.tensor_tensor(f_diag, across(ident[0:HA, 0:HA], NS),
                            fT[:, TP:T].unsqueeze(1).to_broadcast([HA, HA, NS]), ALU.mult)\
                .then_inc(sig("neg_cum"), 1)
            bank = take("f_tok")
            V.tensor_copy(f_tok[:, 0:2, :], bank[:, 0:2 * HA].rearrange("p (t h) -> p t h", h=HA))
            V.tensor_copy(f_tok[0:NS, 2, :], bank[0:NS, 2 * HA:3 * HA])
            give(V.tensor_copy(f_tok[:, 3:5, :], bank[:, 3 * HA:5 * HA].rearrange("p (t h) -> p t h", h=HA)),
                 "f_tok", then_read=True)
            bank = take("new")
            V.tensor_copy(s_new, bank[:, 0:64].rearrange("p (h b) -> p h b", b=NS))
            give(V.tensor_copy(f_new, bank[:, 64:128].rearrange("p (h b) -> p h b", b=NS)), "new")
            dve.wait_ge(sig("tri"), 5)

            def head_mask(h):
                bank = take(f"scores{h}")
                if h >= 2:
                    dve.wait_ge(scalar_full, a_index[f"turned{h - 2}"])
                sc = attn[:, h % 2, :]
                V.scalar_tensor_tensor(out=sc[:, 0:P], in0=bank[:, 0:P], scalar=f_tok[:, 3, h:h + 1],
                                       in1=causal[:, P:2 * P], op0=ALU.subtract, op1=ALU.add)
                give(V.scalar_tensor_tensor(out=sc[:, P:3 * P], in0=bank[:, P:3 * P], scalar=f_tok[:, 4, h:h + 1],
                                            in1=causal[:, :], op0=ALU.subtract, op1=ALU.add),
                     f"scores{h}", then_read=True)
                V.tensor_reduce(row_max[:, 2 * h:2 * h + 1], sc[:, 0:P], AX_X, ALU.max)
                chain(V.tensor_reduce(row_max[:, 2 * h + 1:2 * h + 2], sc[:, P:3 * P], AX_X, ALU.max))
                V.tensor_scalar(row_max[:, 2 * h:2 * h + 2], row_max[:, 2 * h:2 * h + 2], -1.0, None, ALU.mult)\
                    .then_inc(sig("neg_max"), 1)

            def head_norm(h):
                dve.wait_ge(sig("exps"), h + 1)
                sc = attn[:, h % 2, :]
                chain(V.reciprocal(row_inv[:, 2 * h:2 * h + 2], row_sum[:, 2 * h:2 * h + 2]))
                V.tensor_scalar(sc[:, 0:P], sc[:, 0:P], row_inv[:, 2 * h:2 * h + 1], None, ALU.mult)
                V.tensor_scalar(sc[:, P:3 * P], sc[:, P:3 * P], row_inv[:, 2 * h + 1:2 * h + 2], None,
                                ALU.mult).then_inc(sig("probs"), 1)

            for s in range(12):
                if s < HA:
                    head_mask(s)
                if s % 2 == 1 and 3 <= s < HA + 3:
                    i = (s - 3) // 2
                    give(V.tensor_copy(oT[:, i, 0:TP], take(f"o{i}")[:, 0:TP]), f"o{i}")
                if s < HA:
                    head_norm(s)
                keys_half(2 + s // 2, s % 2)

            for i in range(2):
                give(V.tensor_scalar(al_x[:, i, :], take(f"alpha{i}")[:, 0:T], vec["b_alpha"][:, i:i + 1], None,
                                     ALU.add), f"alpha{i}", then_read=True)
            V.scalar_tensor_tensor(out=al_nabs, in0=al_x, scalar=-1.0, in1=al_x, op0=ALU.mult, op1=ALU.min)\
                .then_inc(sig("al_nabs"), 1)
            V.tensor_scalar(al_x, al_x, 0.0, None, ALU.min)
            give(V.tensor_copy(vb_rows, take("vb_rows")[0:NS, :]), "vb_rows")
            give(V.tensor_copy(past_lf, take("past_lf")[:, :].rearrange("p (a j) -> p a j", j=PAGES)), "past_lf",
                 then_read=True)
            dve.wait_ge(sig("al_log"), 1)
            chain(V.tensor_tensor(al_x, al_x, al_nabs, ALU.subtract))
            V.tensor_scalar(la_new, al_x[:, :, TP:T], 1.0 / TAU, None, ALU.mult).then_inc(sig("la_new"), 1)
            chain(V.tensor_scalar(e_q.rearrange("p (i c) t -> p i (c t)", i=2), al_x[:, :, 0:TP], 1.0 / TAU, None,
                                  ALU.mult))
            for ic in range(2 * NCH):
                ins = V.tensor_tensor_scan(al_b[:, ic, :], ones[:, 0:CH], e_q[:, ic, :], 0.0, ALU.mult, ALU.add)
            chain(ins)
            chain(V.tensor_tensor(al_d, al_b, al_b[:, :, CH // 2 - 1:CH // 2].to_broadcast([P, 2 * NCH, CH]),
                                  ALU.subtract))
            V.tensor_scalar(al_d, al_d, EXP_CLAMP, -EXP_CLAMP, ALU.min, ALU.max).then_inc(sig("al_d"), 1)
            give(V.tensor_copy(past_suffix, take("page_sums")[:, :].rearrange("p (a j) -> p a j", j=PAGES)),
                 "page_sums", then_read=True)
            for j in range(PAGES - 2, 0, -1):
                chain(V.tensor_tensor(past_suffix[:, :, j:j + 1], past_suffix[:, :, j:j + 1],
                                      past_suffix[:, :, j + 1:j + 2], ALU.add))
            dve.wait_ge(keys_used, 2 * NS)
            ds_ = dec_scores[:, :, :]
            give(V.tensor_tensor(ds_, ds_, take("in_page_suffix")[:, :].rearrange("p (a j) -> p a j", j=PAGES),
                                 ALU.add), "in_page_suffix", then_read=True)
            chain(V.tensor_tensor(ds_[:, :, 0:PAGES - 1], ds_[:, :, 0:PAGES - 1], past_suffix[:, :, 1:PAGES], ALU.add))
            chain(V.tensor_tensor(ds_, ds_, f_new.rearrange("p h b -> p (h b)").unsqueeze(2)
                                  .to_broadcast([P, HA * NS, PAGES]), ALU.add))
            chain(V.tensor_reduce(dec_max, ds_, AX_X, ALU.max))
            V.tensor_tensor(dec_max, dec_max, s_new.rearrange("p h b -> p (h b)"), ALU.max)\
                .then_inc(sig("dec_max"), 1)
            qb_p = qbT[:, :, 0:TP].rearrange("p i (c t) -> p i c t", t=CH)
            kb_p = kbT[:, :, 0:TP].rearrange("p i (c t) -> p i c t", t=CH)

            def by_tile(ap):
                return ap.rearrange("p (i c) t -> p i c t", i=2)

            dve.wait_ge(sig("al_exp"), 2)
            V.tensor_tensor(by_tile(e_q), by_tile(e_q), qb_p, ALU.mult).then_inc(sig("qg_kg"), 1)
            V.tensor_tensor(by_tile(e_k), by_tile(e_k), kb_p, ALU.mult).then_inc(sig("qg_kg"), 1)
            V.tensor_tensor(al_d, al_b[:, :, CH - 1:CH].to_broadcast([P, 2 * NCH, CH]), al_b, ALU.subtract)\
                .then_inc(sig("al_rest"), 1)
            chain(V.memset(qe, 0.0))
            dve.wait_ge(sig("al_exp"), 3)
            for f in range(2):
                half = slice(64 * f, 64 * f + 64)
                ins = V.tensor_tensor(qe[half, f, :, :].rearrange("p (i c) t -> p i c t", i=2),
                                      by_tile(e_b[half, :, :]), qb_p[half, :, :, :], ALU.mult)
            ins.then_inc(sig("qe"), 1)
            dve.wait_ge(sig("rest_exp"), 1)
            V.tensor_tensor(by_tile(al_d), by_tile(al_d), kb_p, ALU.mult).then_inc(sig("kd"), 1)
            chain(V.memset(A_T, 0.0))
            keep = keep_s_le_t[:, :].bitcast(U32).unsqueeze(1).to_broadcast([CH, NCH, CH])
            for i in range(2):
                for f in range(2):
                    bank = take(f"A{i}{f}")
                    give(V.copy_predicated(A_T[:, i, f, :].rearrange("p (c t) -> p c t", t=CH), keep,
                                           bank[0:CH, 0:TP].rearrange("p (c t) -> p c t", t=CH)), f"A{i}{f}")
            for i in range(2):
                for c2 in range(2):
                    bank = take(f"kv{i}{c2}")
                    for c in (2 * c2, 2 * c2 + 1):
                        for f in range(2):
                            half = slice(64 * f, 64 * f + 64)
                            kv = bank[half, (c % 2) * 256 + f * DV:(c % 2) * 256 + (f + 1) * DV]
                            if c == 0:
                                ins = V.tensor_copy(gla_S[half, 0, i, :], kv)
                            else:
                                ins = V.scalar_tensor_tensor(out=gla_S[half, c, i, :], in0=gla_S[half, c - 1, i, :],
                                                             scalar=e_b[half, i * NCH + c, CH - 1:CH], in1=kv,
                                                             op0=ALU.mult, op1=ALU.add)
                        if c % 2 == 0:
                            chain(ins)
                        elif (i, c2) == (1, 1):
                            give(ins, f"kv{i}{c2}")
                        else:
                            give(ins, f"kv{i}{c2}", then_read=True)
            dve.wait_ge(sig("stored_early"), 16 * 6)
            for h in range(HB):
                give(V.tensor_copy(obT[:, h, 0:TP], take(f"ob{h}")[:, 0:TP]), f"ob{h}")

            state = slot_ap("state")[:, 0:NS * 2 * DV].rearrange("p (b i v) -> p b i v", b=NS, i=2)
            arrived(dve, "state")
            dve.wait_ge(sig("a_new"), 1)
            chain(V.tensor_tensor(state, state, la_new.rearrange("p i b -> p b i").unsqueeze(3)
                                  .to_broadcast([P, NS, 2, DV]), ALU.mult))
            for f in range(2):
                half = slice(64 * f, 64 * f + 64)
                ins = V.tensor_copy(qb_new[half, :, :, f], qbT[half, :, TP:T])
            for b in range(NS):
                bank = take(f"v_row{b}")
                for i in range(2):
                    for f in range(2):
                        half, h = slice(64 * f, 64 * f + 64), 2 * i + f
                        ins = V.scalar_tensor_tensor(out=state[half, b, i, :], in0=bank[half, h * DV:(h + 1) * DV],
                                                     scalar=kbT[half, i, TP + b:TP + b + 1],
                                                     in1=state[half, b, i, :], op0=ALU.mult, op1=ALU.add)
                give(ins, f"v_row{b}")
            bank = take("ob_new")
            give(V.tensor_copy(obT[:, :, TP:T], bank[:, 0:64].rearrange("p (h b) -> p h b", h=4)[:, :, 0:NS]),
                 "ob_new", then_read=True)
            V.tensor_tensor(ob_sq, obT, obT, ALU.mult).then_inc(sig("ob_sq"), 1)
            for h in range(HB):
                give(V.tensor_scalar(ob_rs[:, h, :], take(f"ob_ss{h}")[:, 0:T], 1.0 / DV, EPS, ALU.mult, ALU.add),
                     f"ob_ss{h}", then_read=(h == HB - 1))
            bank = take("dec_maxT")
            give(V.tensor_reduce(dec_m, bank[0:64, 0:P], AX_X, ALU.max), "dec_maxT", then_read=True)
            V.tensor_scalar(dec_diag, ident[0:64, 0:64], dec_m, None, ALU.mult).then_inc(sig("dec_diag"), 1)
            give(V.tensor_copy(dec_top, take("dec_top")[:, 0:64]), "dec_top", then_read=True)
            V.tensor_tensor(ds_, ds_, dec_top.unsqueeze(2).to_broadcast([P, HA * NS, PAGES]), ALU.subtract)
            V.tensor_tensor(s_new, s_new, dec_top.rearrange("p (h b) -> p h b", b=NS), ALU.subtract)\
                .then_inc(sig("dec_shift"), 1)
            dve.wait_ge(sig("ob_rms"), 1)
            chain(V.reciprocal(ob_rs, ob_rs))
            chain(V.tensor_tensor(obT, obT, ob_rs, ALU.mult))
            for h in range(HB):
                ins = V.scalar_tensor_tensor(out=obT[:, h, :], in0=obT[:, h, :], scalar=vec["g_gla"][:, h:h + 1],
                                             in1=rbT[:, h, :], op0=ALU.mult, op1=ALU.mult)
            ins.then_inc(sig("gla_done"), 1)
            bank = take("dec_sums")
            dve.wait_ge(sig("dec_probs"), 1)
            inv = dec_inv.rearrange("p h b -> p (h b)")
            give(V.tensor_reduce(inv, bank[:, :].rearrange("p (a j) -> p a j", j=PAGES), AX_X, ALU.add), "dec_sums",
                 then_read=True)
            chain(V.tensor_tensor(inv, inv, s_new.rearrange("p h b -> p (h b)"), ALU.add))
            chain(V.reciprocal(inv, inv))
            p_new = s_new.rearrange("p (i f) b -> p i f b", f=2)
            inv4 = dec_inv.rearrange("p (i f) b -> p i f b", f=2)
            o_past = ps[:, 7, 0:64].rearrange("p (i b f) -> p i b f", i=4, b=NS)
            for f in range(2):
                half = slice(64 * f, 64 * f + 64)
                ins = V.tensor_tensor(o_new[half, :, :], vT[half, :, TP:T], p_new[half, :, f, :], ALU.mult)
            chain(ins)
            dve.wait_ge(freed[f"V{NS - 1}"][0], freed[f"V{NS - 1}"][1])
            for f in range(2):
                half = slice(64 * f, 64 * f + 64)
                ins = V.tensor_tensor(o_new[half, :, :], o_new[half, :, :], o_past[half, :, :, f], ALU.add)
            chain(ins)
            for f in range(2):
                half = slice(64 * f, 64 * f + 64)
                ins = V.tensor_tensor(oT[half, :, TP:T], o_new[half, :, :], inv4[half, :, f, :], ALU.mult)
            ins.then_inc(sig("oT"), 1)

            modulation(1)
            modulation(2)
            for m in range(KT):
                dve.wait_ge(scalar_free, a_index["gb1_3"])
                give(V.tensor_tensor(hT[:, m, :], take(f"y0_{m}")[:, 0:T], gaT[:, m, :], ALU.mult), f"y0_{m}")
                give(V.tensor_tensor(gbT[:, m, :], take(f"y1_{m}")[:, 0:T], gbT[:, m, :], ALU.mult), f"y1_{m}",
                     then_read=True)
                ins = V.tensor_tensor(hT[:, m, :], hT[:, m, :], gbT[:, m, :], ALU.add)
            ins.then_inc(sig("mixed"), 1)

            def residual(m, branch, gate, done, sample_tmp):
                V.tensor_tensor(sample_tmp, branch[:, TP:T], modT[:, gate + m, 1:9], ALU.mult)
                done(V.scalar_tensor_tensor(out=xT[:, m, 0:TP], in0=branch[:, 0:TP], scalar=modT[:, gate + m, 0:1],
                                            in1=xT[:, m, 0:TP], op0=ALU.mult, op1=ALU.add))
                return V.tensor_tensor(xT[:, m, TP:T], xT[:, m, TP:T], sample_tmp, ALU.add)

            for m in range(KT):
                ins = residual(m, take(f"out{m}")[:, 0:T], 16,
                               lambda i, m=m: give(i, f"out{m}", then_read=True), o_new[:, m % 4, :])
            ins.then_inc(sig("x1"), 1)

            def rms_row(name, rms_ready):
                give(V.tensor_scalar(row_t, take(name)[:, 0:T], 1.0 / D, EPS, ALU.mult, ALU.add), name,
                     then_read=True)
                dve.wait_ge(sig(rms_ready), 1)
                chain(V.reciprocal(row_t, row_t))

            rms_row("x1_ss", "x1_rms")
            normed(gain2, 24, "g_ffn", 32).then_inc(sig("h2T"), 1)

            bank = take("logits")
            dve.wait_ge(sig("b_r"), 16)
            for t, (t0, tn) in enumerate(TOK_TILES):
                ins = V.tensor_tensor(logits[0:tn, t, :], bank[0:tn, t * NE:(t + 1) * NE], b_r[0:tn, :], ALU.add)
            give(ins, "logits", then_read=True)
            for t, (t0, tn) in enumerate(TOK_TILES):
                lg = logits[0:tn, t, :]
                chain(V.max(out=top8[0:tn, t, :], in_=lg))
                V.tensor_copy(keys8[0:tn, t, 0:4], top8[0:tn, t, 0:4])
                chain(V.tensor_copy(keys8[0:tn, t, 4:8], top8[0:tn, t, 0:1].to_broadcast([tn, 4])))
                chain(V.match_replace(out=rest[0:tn, t, :], in_to_replace=keys8[0:tn, t, :], in_values=lg,
                                      imm_value=NEG))
                V.tensor_tensor(chosen[0:tn, t, :], rest[0:tn, t, :], lg, ALU.not_equal)\
                    .then_inc(sig("chosen"), 1)
                V.tensor_scalar(keys8[0:tn, t, 7:8], top8[0:tn, t, 0:1], -1.0, None, ALU.mult)\
                    .then_inc(sig("top_neg"), 1)
            for t, (t0, tn) in enumerate(TOK_TILES):
                dve.wait_ge(sig("top_exp"), t + 1)
                g = gates[0:tn, t, :]
                chain(V.tensor_tensor(g, logits[0:tn, t, :], chosen[0:tn, t, :], ALU.mult))
                chain(V.tensor_reduce(rstd[0:tn, t:t + 1], g, AX_X, ALU.add))
                chain(V.reciprocal(rstd[0:tn, t:t + 1], rstd[0:tn, t:t + 1]))
                V.tensor_scalar(g, g, rstd[0:tn, t:t + 1], None, ALU.mult).then_inc(sig("gates"), 1)
            bank = take("places")
            chain(V.tensor_reduce(rounds_f[:, 0:1], bank[:, 3 * NE:4 * NE], AX_X, ALU.max))
            for t, (t0, tn) in enumerate(TOK_TILES):
                ins = V.scalar_tensor_tensor(out=place[0:tn, t, :], in0=bank[0:tn, t * NE:(t + 1) * NE], scalar=1.0,
                                             in1=chosen[0:tn, t, :], op0=ALU.add, op1=ALU.mult)
            give(ins, "places", then_read=True)
            for t, (t0, tn) in enumerate(TOK_TILES):
                ins = V.tensor_scalar(place[0:tn, t, :], place[0:tn, t, :], -1.0, None, ALU.add)
            chain(ins)
            thresholds = rest[:, 0, 0:MAX_ROUNDS - 1]
            for r in range(1, MAX_ROUNDS):
                ins = V.tensor_scalar(thresholds[:, r - 1:r], rounds_f[:, 0:1], float(CAP * r), None, ALU.is_gt)
            chain(ins)
            chain(V.tensor_reduce(rounds_f[:, 1:2], thresholds, AX_X, ALU.add))
            V.tensor_scalar(rounds_i[0:1, 0:1], rounds_f[0:1, 1:2], 1.0, None, ALU.add).then_inc(sig("rounds"), 1)

            def set_pick(n, p):
                for j in range(2):
                    V.tensor_copy(expert_row[:, j, :],
                                  ident[0:NE, bass.ds(2 * p + j, 1)].to_broadcast([NE, CAP]))
                    for t, (t0, tn) in enumerate(TOK_TILES):
                        ins = V.tensor_scalar(pick[0:tn, t, j * CAP:(j + 1) * CAP], slots_iota[0:tn, :],
                                              place[0:tn, t, bass.ds(2 * p + j, 1)], None, ALU.is_equal)
                ins.then_inc(sig("pick_ready"), 1)

            def set_put(n, p):
                for j in range(2):
                    for t, (t0, tn) in enumerate(TOK_TILES):
                        ins = V.tensor_scalar(put[0:tn, t, j * CAP:(j + 1) * CAP], slots_iota[0:tn, :],
                                              place[0:tn, t, bass.ds(2 * p + j, 1)],
                                              gates[0:tn, t, bass.ds(2 * p + j, 1)], ALU.is_equal, ALU.mult)
                ins.then_inc(sig("put_ready"), 1)

            def swiglu(n, j, first):
                e = 2 * n + j
                dve.wait_ge(sig("slots_used"), gu_done(n, j, first))
                V.tensor_scalar(gate_v, ps[0:CAP, 2 * j:2 * j + 2, :].rearrange("p a b -> p (a b)"),
                                LIMIT, None, ALU.min).then_inc(sig("gate_ready"), 1)
                V.tensor_scalar(hid, ps[64:64 + CAP, 2 * j:2 * j + 2, :].rearrange("p a b -> p (a b)"),
                                LIMIT, -LIMIT, ALU.min, ALU.max).then_inc(sig("up_clipped"), 1)
                dve.wait_ge(sig("up_clipped"), e + 1)
                V.scalar_tensor_tensor(out=hid, in0=hid, scalar=1.0, in1=gate_v, op0=ALU.add, op1=ALU.mult)\
                    .then_inc(sig("up_times_gate"), 1)
                dve.wait_ge(sig("up_times_gate"), e + 1)
                dve.wait_ge(sig("sig_ready"), e + 1)
                V.tensor_tensor(hid, hid, sig_v, ALU.mult).then_inc(sig("hid_ready"), 1)

            def add_pair(n):
                for m in range(KT):
                    dve.wait_ge(sig("combined"), n * KT + m + 1)
                    V.tensor_tensor(acc[:, m, :], acc[:, m, :], ps[:, 6 + m % 2, 0:T], ALU.add)\
                        .then_inc(sig("added"), 1)

            def pair(n, p, first, last):
                swiglu(n, 0, first)
                if not last:
                    dve.wait_ge(sig("slots_used"), n * 12 + 5)
                    set_pick(n + 1, p + 1)
                set_put(n, p)
                if not first:
                    add_pair(n - 1)
                swiglu(n, 1, False)

            def one_round(rnd):
                n = rnd * PAIRS
                if not isinstance(rnd, int):
                    for t, (t0, tn) in enumerate(TOK_TILES):
                        ins = V.tensor_scalar(place[0:tn, t, :], place[0:tn, t, :], float(-CAP), None, ALU.add)
                    ins.then_inc(sig("moved_up"), 1)
                    dve.wait_ge(sig("moved_up"), rnd)
                set_pick(n, 0)
                pair(n, 0, True, False)
                with dve.Fori(1, PAIRS - 1) as p:
                    pair(n + p, p, False, False)
                pair(n + (PAIRS - 1), PAIRS - 1, False, True)
                add_pair(n + (PAIRS - 1))

            give(V.tensor_copy(gatesT, take("gatesT")[0:NE, 0:T]), "gatesT")
            for m in range(KT):
                give(V.tensor_copy(acc[:, m, :], take(f"bias{m}")[:, 0:T]), f"bias{m}", then_read=(m == KT - 1))
            one_round(0)
            dve.wait_ge(sig("rounds"), 1)
            rounds = dve.value_load(rounds_i[0:1, 0:1], min_val=1, max_val=MAX_ROUNDS)
            with dve.If(rounds > 1):
                with dve.Fori(1, rounds) as rnd:
                    one_round(rnd)

            dve.wait_ge(sig("added"), PAIRS * KT)
            for m in range(KT):
                ins = residual(m, acc[:, m, :], 40, chain, o_new[:, m % 4, :])
            ins.then_inc(sig("x2"), 1)
            rms_row("x2_ss", "x2_rms")
            chain(V.tensor_tensor(hT[:, :, :], xT[:, :, :], row_t.unsqueeze(1).to_broadcast([P, KT, T]), ALU.mult))
            for k in range(KT):
                ins = V.tensor_scalar(hT[:, k, :], hT[:, k, :], vec["g_final"][:, k:k + 1], None, ALU.mult)
            ins.then_inc(sig("yT"), 1)

        @block.sync
        def _(sp):
            for b in range(NS):
                freed[f"K{b}"] = (keys_used, 2 * (b + 1))
            loaded_pages = [False]

            def load(item):
                n = ITEMS.index(item)
                if n >= SLOTS:
                    before_ = ITEMS[n - SLOTS]
                    sp.wait_ge(*freed[before_])
                    if before_ == "state":
                        sp.wait_ge(sig("state_stored"), 16)
                s, _ = landing[item]
                dst = ring[:, s, :]
                if item[0:3] == "ada":
                    a = int(item[3:])
                    part_no, kp = a // 4, a % 4
                    sp.dma_start(dst[:, 0:4096].rearrange("p (k c) -> p k c", k=2),
                                 w_ada[0].rearrange("(k p) c -> p k c", p=P)[
                                     :, 2 * kp:2 * kp + 2, part_no * 2048:(part_no + 1) * 2048])\
                        .then_inc(landed[s], 16)
                elif item in WIN:
                    c0, n_cols = WIN[item]
                    sp.dma_start(dst[:, 0:n_cols * KT].rearrange("p (k c) -> p k c", k=KT),
                                 w_in[0].rearrange("(k p) c -> p k c", p=P)[:, :, c0:c0 + n_cols])\
                        .then_inc(landed[s], 16)
                elif item[0] in "KV":
                    b = int(item[1:])
                    if not loaded_pages[0]:
                        sp.wait_ge(sig("pages"), 32)
                        loaded_pages[0] = True
                    cache = cache_k if item[0] == "K" else cache_v
                    rows = cache[0].rearrange("n s h d -> n s (h d)")
                    with sp.Fori(0, PAGES) as j:
                        page = sp.value_load(pages_row[0:1, bass.ds(b * PAGES + j, 1)], min_val=0,
                                             max_val=N_PHYS - 1)
                        sp.dma_start(dst[:, bass.ds(j * WA, WA)],
                                     rows[bass.ds(page, 1), :, :].rearrange("a s c -> (a s) c"))\
                            .then_inc(landed[s], 16)
                elif item == "state":
                    sp.dma_start(dst[:, 0:NS * 2 * DV].rearrange("p (a v) -> p a v", v=DV),
                                 state_gla[0].rearrange("b (i f) k v -> (f k) (b i) v", f=2))\
                        .then_inc(landed[s], 16)
                else:
                    w = w_branch if item[1] == "b" else w_o
                    r = int(item[2:])
                    sp.dma_start(dst[:, 0:4096].rearrange("p (k c) -> p k c", k=4),
                                 w[0].rearrange("(k p) c -> p k c", p=P)[:, 4 * r:4 * r + 4, :])\
                        .then_inc(landed[s], 16)

            def store(dst, src):
                sp.dma_start(dst, src).then_inc(sig("stored_early"), 16)

            for item in ITEMS:
                load(item)
                if item == "K2":
                    sp.wait_ge(vector_free, v_index["f_tok"])
                    for src, new, d_p, d_s in ((k_tok, k_new_rows, k_prompt, k_sample),
                                               (v_tok, v_new_rows, v_prompt, v_sample)):
                        store(d_p[0, 0].rearrange("(t p) h d -> p t (h d)", p=P), src[:, 0:2, :])
                        store(d_s[0].rearrange("b s h d -> (b s) (h d)"), new)
                    store(logf_prompt[0, 0].rearrange("(t p) h -> p t h", p=P), f_tok[:, 0:2, :])
                    store(logf_sample[0].rearrange("b s h -> (b s) h"), f_tok[0:NS, 2, :])

            gu = w_gu[0].rearrange("e (k p) c -> e p k c", p=P)
            dn = w_d[0].rearrange("e (k p) c -> e p k c", p=P)

            def load_expert(kind, e, number, edge, phase_one=False):
                for s in range(4 if kind == "gu" else 2):
                    slot, _ = expert_landing(kind, s, 0, edge)
                    if phase_one and number + s < SLOTS:
                        sp.wait_ge(*freed[ITEMS[len(ITEMS) - SLOTS + number + s]])
                    else:
                        sp.wait_ge(sig("slots_used"), number + (s + 1 - SLOTS))
                    if kind == "gu":
                        src, k = gu[bass.ds(e, 1), :, 2 * s:2 * s + 2, :], 2
                    else:
                        src, k = dn[bass.ds(e, 1), :, 4 * s:4 * s + 4, :], 4
                    sp.dma_start(ring[:, slot, 0:4096].rearrange("p (k c) -> p k c", k=k),
                                 src.rearrange("e p k c -> (e p) k c")).then_inc(landed[slot], 16)

            def load_round(rnd):
                start, phase_one = rnd * (SLOTS * NE), isinstance(rnd, int)
                load_expert("gu", 0, start, True, phase_one)
                load_expert("gu", 1, start + 4, False, phase_one)
                load_expert("dn", 0, start + 8, False)
                with sp.Fori(1, NE - 1) as e:
                    load_expert("gu", e + 1, start + e * SLOTS + 4, False)
                    load_expert("dn", e, start + e * SLOTS + 8, False)
                load_expert("dn", NE - 1, start + SLOTS * NE - 2, True)

            load_round(0)
            sp.wait_ge(sig("rounds"), 1)
            rounds = sp.value_load(rounds_i[0:1, 0:1], min_val=1, max_val=MAX_ROUNDS)
            with sp.If(rounds > 1):
                with sp.Fori(1, rounds) as rnd:
                    load_round(rnd)
            sp.wait_ge(sig("stored_early"), 16 * 6)

        @block.gpsimd
        def _(pool):
            nc.gpsimd.memset(ident[:, :], 0.0).then_inc(gstep, 1)
            nc.gpsimd.memset(ones[:, :], 1.0).then_inc(sig("ones"), 1)
            nc.gpsimd.memset(causal[:, :], 0.0).then_inc(gstep, 1)
            pool.wait_ge(gstep, 2)
            pool.wait_ge(sig("ones"), 1)
            nc.gpsimd.affine_select(out=ident[:, :], in_=ident[:, :], compare_op=ALU.not_equal, fill=1.0,
                                    base=0, pattern=[[-1, P]], channel_multiplier=1).then_inc(sig("ident"), 1)
            nc.gpsimd.affine_select(out=before[:, :], in_=ones[:, :], compare_op=ALU.is_gt, fill=0.0,
                                    base=0, pattern=[[1, P]], channel_multiplier=-1).then_inc(sig("tri"), 1)
            nc.gpsimd.affine_select(out=after[:, :], in_=ones[:, :], compare_op=ALU.is_gt, fill=0.0,
                                    base=0, pattern=[[-1, P]], channel_multiplier=1).then_inc(sig("tri"), 1)
            nc.gpsimd.affine_select(out=causal[:, P:2 * P], in_=causal[:, P:2 * P], compare_op=ALU.is_ge,
                                    fill=NEG, base=0, pattern=[[-1, P]], channel_multiplier=1)\
                .then_inc(sig("tri"), 1)
            nc.gpsimd.affine_select(out=keep_s_le_t[:, :], in_=ones[0:CH, 0:CH], compare_op=ALU.is_ge,
                                    fill=0.0, base=0, pattern=[[1, CH]], channel_multiplier=-1)\
                .then_inc(sig("tri"), 1)
            nc.gpsimd.iota(slots_iota[:, :], pattern=[[1, CAP]], base=0, channel_multiplier=0,
                           allow_small_or_imprecise_dtypes=True).then_inc(sig("tri"), 1)
            pool.wait_ge(sig("pages"), 32)
            nc.gpsimd.indirect_dma_start(
                out=lf_rows, out_offset=None, in_=cache_logf[0].rearrange("n s h -> n (s h)"),
                in_offset=bass.IndirectOffsetOnAxis(ap=pages_col[:, 0:1].bitcast(U32), axis=0)).then_inc(sig("lf_rows"), 16)
            pool.wait_ge(vector_free, v_index["kv11"])
            for i in range(2):
                nc.gpsimd.dma_start(gla_prompt[0, 0, 2 * i:2 * i + 2].rearrange("f k v -> (f k) v"),
                                    gla_S[:, NCH - 1, i, :]).then_inc(sig("gla_stored"), 16)
            pool.wait_ge(vector_free, v_index[f"v_row{NS - 1}"])
            nc.gpsimd.dma_start(gla_sample[0].rearrange("b (i f) k v -> (f k) (b i) v", f=2),
                                slot_ap("state")[:, 0:NS * 2 * DV].rearrange("p (a v) -> p a v", v=DV))\
                .then_inc(sig("state_stored"), 16)
            pool.wait_ge(sig("mixed"), 1)
            nc.gpsimd.dma_start(b_gu_rows, b_gu[0]).then_inc(sig("b_gu_rows"), 16)
            nc.gpsimd.dma_start(w_r, w_router[0].rearrange("(k p) e -> p k e", p=P)).then_inc(sig("w_r"), 16)
            nc.gpsimd.dma_start(b_d_sb, b_d[0]).then_inc(sig("b_d"), 16)
            nc.gpsimd.dma_start(b_r, b_router[0].partition_broadcast(P)).then_inc(sig("b_r"), 16)
            pool.wait_ge(sig("gla_stored"), 32)
            pool.wait_ge(sig("state_stored"), 16)


_INS = ["x_prompt", "x_sample", "c_prompt", "c_sample", "cache_k", "cache_v", "cache_logf", "state_gla",
        "page_table", "g_mix", "g_ffn", "g_final", "w_ada", "b_ada", "w_in", "b_f", "w_alpha", "b_alpha",
        "g_gla", "w_branch", "w_o", "w_router", "b_router", "w_gu", "b_gu", "w_d", "b_d"]
_OUTS = [(1, TP, D), (NS, 1, D), (1, 1, TP, HA, DH), (1, 1, TP, HA, DH), (1, 1, TP, HA), (1, 1, HB, DK, DV),
         (1, NS, 1, HA, DH), (1, NS, 1, HA, DH), (1, NS, 1, HA), (1, NS, HB, DK, DV)]


def kernel(**inputs):
    import concourse.bacc as bacc
    from concourse.bass_utils import run_bass_kernel_spmd

    nc = bacc.Bacc("TRN2", target_bir_lowering=False, num_devices=1)
    arrays, args = {}, []
    for name in _INS:
        a = np.ascontiguousarray(inputs[name])
        arrays[f"in_{name}"] = a
        args.append(nc.dram_tensor(f"in_{name}", a.shape, mybir.dt.from_np(a.dtype), kind="ExternalInput").ap())
    for i, shape in enumerate(_OUTS):
        args.append(nc.dram_tensor(f"out_{i}", shape, F32, kind="ExternalOutput").ap())
    decoder_step(nc, *args)
    r = run_bass_kernel_spmd(nc, [arrays], core_ids=[0])
    return tuple(r.results[0][f"out_{i}"] for i in range(len(_OUTS)))
```

```python
from contextlib import ExitStack

import concourse.bass as bass
import numpy as np
from concourse import mybir

F32 = mybir.dt.float32
I32 = mybir.dt.int32
U32 = mybir.dt.uint32
ALU = mybir.AluOpType
ACT = mybir.ActivationFunctionType
AX_X = mybir.AxisListType.X

P = 128
D = 1024
KT = D // P
TP = 256
NS = 8
T = TP + NS
HA, DH = 8, 64
WA = HA * DH
HB, DK, DV = 4, 64, 128
CH = 64
NCH = TP // CH
PAGES, PAGE, N_PHYS = 8, 128, 80
NE, TOPK, FF = 32, 4, 1024
CAP = 64
PAIRS = NE // 2
MAX_ROUNDS = -(-T // CAP)
EPS = 1e-6
LIMIT, ALPHA = 7.0, 1.702
SCALE = DH ** -0.5
TAU = 16.0
NEG = -1e30
EXP_CLAMP = 80.0

QA, KA, VA, FA = 0, 512, 1024, 1536
QB, KB, VB = 1544, 1800, 2056
RB, ALR, GA, GB = 2568, 3080, 3096, 4120

TOK_TILES = [(0, 128), (128, 128), (256, 8)]

ITEMS = (["ada0", "ada1", "ada2", "ada3", "qa", "ka", "va", "fqk", "K0", "K1", "vb", "K2", "K3", "rb"]
         + ["K4", "K5", "K6", "K7", "ada4", "ada5", "ada6", "ada7", "state", "ga0", "ga1", "V0", "V1",
            "gb0", "V2", "V3", "gb1", "V4", "V5", "V6", "V7", "ada8", "ada9", "ada10", "ada11"]
         + ["wb0", "wb1", "wo0", "wo1"])
WIN = {"qa": (QA, 512), "ka": (KA, 512), "va": (VA, 512), "fqk": (FA, 520), "vb": (VB, 512),
       "rb": (RB, 528), "ga0": (GA, 512), "ga1": (GA + 512, 512), "gb0": (GB, 512), "gb1": (GB + 512, 512)}
SLOTS = 6
SLOT = 528 * KT
EXPERT_SLOTS = [(len(ITEMS) + s) % SLOTS for s in range(SLOTS)]

VEC_ROWS = {"b_ada": (0, 48), "g_mix": (48, 8), "g_ffn": (56, 8), "g_final": (64, 8), "g_gla": (72, 4),
            "b_alpha": (76, 2)}
N_VEC = 78
N_SMALL = 800


def decoder_step(nc, x_prompt, x_sample, c_prompt, c_sample, cache_k, cache_v, cache_logf, state_gla,
                 page_table, g_mix, g_ffn, g_final, w_ada, b_ada, w_in, b_f, w_alpha, b_alpha, g_gla,
                 w_branch, w_o, w_router, b_router, w_gu, b_gu, w_d, b_d,
                 y_prompt, y_sample, k_prompt, v_prompt, logf_prompt, gla_prompt,
                 k_sample, v_sample, logf_sample, gla_sample):
    with ExitStack() as ctx:
        def sb(name, shape, dt=F32):
            return ctx.enter_context(nc.sbuf_tensor(name, shape, dt))

        def sem(name):
            return ctx.enter_context(nc.semaphore(name))

        ps = ctx.enter_context(nc.psum_tensor("ps", [P, 8, 512], F32))
        ring = sb("ring", [P, SLOTS, SLOT])
        ident = sb("ident", [P, P])
        ones = sb("ones", [P, P])
        before = sb("before", [P, P])
        after = sb("after", [P, P])
        causal = sb("causal", [P, 2 * P])
        keep_s_le_t = sb("keep_s_le_t", [CH, CH])
        slots_iota = sb("slots_iota", [P, CAP])
        vecT = sb("vecT", [P, N_VEC])
        b_f_col = sb("b_f_col", [HA, 1])
        w_alpha_sb = sb("w_alpha_sb", [16, 256])
        pages_row = sb("pages_row", [1, NS * PAGES], I32)
        pages_col = sb("pages_col", [NS * PAGES, 1], I32)
        modT = sb("modT", [P, 48, 9])
        cT = sb("cT", [P, KT, 32])
        gain1 = sb("gain1", [P, KT, 9])
        gain2 = sb("gain2", [P, KT, 9])
        xT = sb("xT", [P, KT, T])
        hT = sb("hT", [P, KT, T])
        tok = sb("tok", [P, 3, D])
        zone = sb("zone", [P, 10560])
        k_tok = sb("k_tok", [P, 3, WA])
        v_tok = sb("v_tok", [P, 2, WA])
        oT = sb("oT", [P, 4, T])
        attn = sb("attn", [P, 4, 384])
        gla_S = sb("gla_S", [P, NCH, 2, DV])
        neg_cum = sb("neg_cum", [P, T])
        f_tok = sb("f_tok", [P, 5, HA])
        dec_scores = sb("dec_scores", [P, HA * NS, PAGES])
        small = sb("small", [P, N_SMALL])

        def part(base, rows, off, *dims):
            n = int(np.prod(dims))
            ap = base[rows, off:off + n]
            if len(dims) == 2:
                return ap.rearrange("p (a b) -> p a b", b=dims[1])
            if len(dims) == 3:
                return ap.rearrange("p (a b c) -> p a b c", b=dims[1], c=dims[2])
            return ap

        ALLP = slice(0, P)
        qT = part(zone, ALLP, 0, 4, T)
        kT = part(zone, ALLP, 1056, 4, T)
        vT = part(zone, ALLP, 2112, 4, T)
        qbT = part(zone, ALLP, 3168, 2, T)
        kbT = part(zone, ALLP, 3696, 2, T)
        vbT = part(zone, ALLP, 4224, 4, T)
        rbT = part(zone, ALLP, 5280, 4, T)
        gaT = part(zone, ALLP, 6336, KT, T)
        gbT = part(zone, ALLP, 8448, KT, T)
        past_lf = part(zone, ALLP, 1056, HA * NS, PAGES)
        past_suffix = part(zone, ALLP, 1568, HA * NS, PAGES)
        mod_rows = part(zone, ALLP, 4224, 512)
        vec_rows = part(zone, slice(0, N_VEC), 0, P)
        k_new_rows, v_new_rows = k_tok[0:NS, 2, :], k_tok[32:32 + NS, 2, :]
        fT = part(zone, slice(0, HA), 6336, T)
        f_nabs = part(zone, slice(0, HA), 7888, T)
        alrT = part(zone, slice(0, 16), 7888, T)
        al_x = part(zone, ALLP, 6336, 2, T)
        al_d = part(zone, ALLP, 6864, 2 * NCH, CH)
        al_b = part(zone, ALLP, 7376, 2 * NCH, CH)
        e_q = part(zone, ALLP, 7888, 2 * NCH, CH)
        e_k = part(zone, ALLP, 8400, 2 * NCH, CH)
        e_b = part(zone, ALLP, 8912, 2 * NCH, CH)
        q_rows = part(zone, slice(0, NS), 9936, WA)
        qe = part(zone, ALLP, 9424, 2, 2 * NCH, CH)
        masked = tok[:, 0, :].rearrange("p (n c) -> p n c", n=2)
        kd_tok = tok[0:CH, 0, :].rearrange("p (i c k) -> p i c k", i=2, c=NCH)
        vb_tok = tok[0:CH, 1:3, :].rearrange("p a (c v) -> p (a c) v", v=HB * DV)
        c_rows = hT[0:9, :, :].rearrange("p a b -> p (a b)")[:, 0:D]
        junk = hT[:, :, :].rearrange("p a b -> p (a b)")[:, D + 64:2 * D + 64]
        rstd_diag = attn[:, 0, :].rearrange("p (t c) -> p t c", t=3)
        al_nabs = part(zone, ALLP, 8400, 2, T)
        ob_sq = part(zone, ALLP, 1056, 4, T)
        ob_rs = part(zone, ALLP, 0, 4, T)
        obT = k_tok[:, :, :].rearrange("p a b -> p (a b)")[:, 0:4 * T].rearrange("p (h t) -> p h t", h=4)
        attn_flat = attn[:, :, :].rearrange("p a b -> p (a b)")
        A_T = attn_flat[0:CH, 0:1024].rearrange("p (i f c t) -> p i f (c t)", i=2, f=2, c=NCH)
        vb_rows = attn_flat[0:NS, 1024:1536]
        o_rows = vb_rows
        lf_rows = gla_S[0:NS * PAGES, :, :, :].rearrange("p a b c -> p (a b c)")
        acc = part(zone, ALLP, 0, KT, T)
        xg = part(zone, ALLP, 2112, KT, 2 * CAP)
        gate_v = part(zone, slice(0, CAP), 3136, FF)
        hid = part(zone, slice(0, CAP), 4160, FF)
        b_d_sb = part(zone, slice(0, NE), 5184, D)
        pick = part(zone, ALLP, 6336, 3, 2 * CAP)
        put = part(zone, ALLP, 6720, 3, 2 * CAP)
        putT = part(zone, ALLP, 7104, T)
        expert_row = part(zone, slice(0, NE), 7368, 2, CAP)
        b_gu_rows = part(zone, slice(0, NE), 7496, 2 * FF)
        place = part(zone, ALLP, 9928, 3, NE)
        gates = part(zone, ALLP, 10024, 3, NE)
        w_r = part(zone, ALLP, 10120, KT, NE)
        gatesT = part(zone, slice(0, NE), 9544, T)
        logitsT = gatesT
        sq_zone = part(zone, ALLP, 0, KT, T)
        hidT = oT[:, :, :].rearrange("p a b -> p (a b)")[:, 0:KT * CAP].rearrange("p (k c) -> p k c", c=CAP)
        sig_v = k_tok[0:CAP, :, :].rearrange("p a b -> p (a b)")[:, 0:FF]
        ye_tok = v_tok[:, :, :].rearrange("p a b -> p (a b)")

        at = [0]

        def tiny(rows, *dims):
            off = at[0]
            at[0] += int(np.prod(dims))
            assert at[0] <= N_SMALL, at[0]
            return part(small, slice(0, rows), off, *dims)

        ssq = tiny(P, 3)
        rstd = tiny(P, 3)
        row_max = tiny(P, 16)
        row_sum = tiny(P, 16)
        row_inv = tiny(P, 16)
        b_last = tiny(P, 2 * NCH)
        la_new = tiny(P, 2, NS)
        qb_new = tiny(P, 2, NS, 2)
        qk_new = tiny(P, HA, NS)
        s_new = tiny(P, HA, NS)
        f_diag = tiny(NS, HA, NS)
        f_new = tiny(P, HA, NS)
        dec_max = tiny(P, HA * NS)
        dec_top = tiny(P, HA * NS)
        dec_diag = tiny(HA * NS, HA * NS)
        dec_inv = tiny(P, HA, NS)
        o_new = tiny(P, 4, NS)
        dec_m = tiny(HA * NS, 1)
        head_of_row = tiny(P, HA)
        to_row = tiny(P, NS, NS)
        logits = part(attn_flat, ALLP, 1024, 3, NE)
        rest = part(attn_flat, ALLP, 1120, 3, NE)
        chosen = part(attn_flat, ALLP, 1216, 3, NE)
        top8 = part(attn_flat, ALLP, 1312, 3, 8)
        keys8 = part(attn_flat, ALLP, 1336, 3, 8)
        b_r = part(attn_flat, ALLP, 1360, NE)
        rounds_f = tiny(P, 2)
        rounds_i = sb("rounds_i", [1, 1], I32)
        row_t = attn_flat[:, 384:384 + T]

        landed = [sem(f"landed{s}") for s in range(SLOTS)]
        items_used = sem("items_used")
        keys_used = sem("keys_used")
        vector_full, vector_free = sem("vector_full"), sem("vector_free")
        scalar_full, scalar_free = sem("scalar_full"), sem("scalar_free")
        query_full, query_free = sem("query_full"), sem("query_free")
        vstep, astep, gstep = sem("vstep"), sem("astep"), sem("gstep")
        named = {}

        def sig(name):
            if name not in named:
                named[name] = sem("s_" + name)
            return named[name]

        v_index, a_index, q_index = {}, {}, {}
        freed = {}
        slot_count = [0] * SLOTS
        landing = {}
        for n, item in enumerate(ITEMS):
            s = n % SLOTS
            slot_count[s] += 16 * (PAGES if item[0] == "K" else PAGES // 2 if item[0] == "V" else 1)
            landing[item] = (s, slot_count[s])

        def slot_ap(item):
            return ring[:, landing[item][0], :]

        def arrived(eng, item):
            eng.wait_ge(landed[landing[item][0]], landing[item][1])

        def gu_done(n, j, first):
            return n * 12 + (8 if j else 4 if first else 2)

        def down_done(n, j, last):
            return n * 12 + (10 if j == 0 else 12 if last else 16)

        def expert_landing(kind, s, e, edge):
            if kind == "gu":
                slot, value = (s, e + 1) if edge else (4 + s, e) if s < 2 else (s - 2, e + 1)
            else:
                slot, value = (4 + s, e + 1) if edge else (2 + s, e + 2)
            slot = EXPERT_SLOTS[slot]
            return slot, value * 16 + slot_count[slot]

        def load_pages(eng, item, half, done):
            b, slot = int(item[1:]), landing[item][0]
            rows = (cache_k if item[0] == "K" else cache_v)[0].rearrange("n s h d -> n s (h d)")
            order = range(half * PAGES // 2, (half + 1) * PAGES // 2)
            pages = [eng.value_load(pages_row[0:1, b * PAGES + j:b * PAGES + j + 1], min_val=0, max_val=N_PHYS - 1)
                     for j in order]
            for j, page in zip(order, pages):
                eng.dma_start(ring[:, slot, j * WA:(j + 1) * WA],
                              rows[bass.ds(page, 1), :, :].rearrange("a s c -> (a s) c")).then_inc(done, 16)

        block = ctx.enter_context(nc.Block())

        @block.tensor
        def _(pe):
            def vector_bank():
                n = len(v_index)
                if n >= 3:
                    pe.wait_ge(vector_free, n - 2)
                return ps[:, 2 + n % 3, :]

            def vector_filled(ins, name):
                ins.then_inc(vector_full, 1)
                v_index[name] = len(v_index) + 1

            def scalar_bank():
                n = len(a_index)
                if n >= 2:
                    pe.wait_ge(scalar_free, n - 1)
                return ps[:, n % 2, :]

            def scalar_filled(ins, name):
                ins.then_inc(scalar_full, 1)
                a_index[name] = len(a_index) + 1

            def from_vector(name):
                pe.wait_ge(vector_free, v_index[name])

            def from_scalar(name):
                pe.wait_ge(scalar_free, a_index[name])

            used = [0]

            def release(ins, item):
                ins.then_inc(items_used, 1)
                used[0] += 1
                freed[item] = (items_used, used[0])

            def transpose(out, in_):
                n = in_.shape[0]
                return pe.transpose(out, in_, ident[0:n, 0:n])

            pe.wait_ge(sig("ones"), 1)
            pe.wait_ge(sig("ident"), 1)
            pe.wait_ge(sig("vec_rows"), 16 * len(VEC_ROWS))
            bank = vector_bank()
            vector_filled(transpose(bank[:, 0:N_VEC], vec_rows), "vectors")
            pe.wait_ge(sig("c_silu"), 1)
            bank = vector_bank()
            for k in range(KT):
                ins = transpose(bank[:, 9 * k:9 * k + 9], c_rows[:, k * P:(k + 1) * P])
            vector_filled(ins, "cT")
            pe.wait_ge(sig("x_tok"), 32)
            for k in range(KT):
                bank = vector_bank()
                for t, (t0, tn) in enumerate(TOK_TILES):
                    ins = transpose(bank[:, t0:t0 + tn], tok[0:tn, t, k * P:(k + 1) * P])
                vector_filled(ins, f"xT{k}")

            def modulate(first, bank, n_parts):
                for n in n_parts:
                    item = f"ada{first + n}"
                    arrived(pe, item)
                    w = slot_ap(item)[:, 0:4096].rearrange("p (k c) -> p k c", k=2)
                    for kk in range(2):
                        for q in range(4):
                            ins = pe.matmul(bank[32 * q:32 * q + 32, :], cT[:, 2 * n + kk, :],
                                            w[:, kk, q * 512:(q + 1) * 512], start=(n == 0 and kk == 0),
                                            stop=(n == 3 and kk == 1), skip_group_check=True)
                    if n < 3:
                        release(ins, item)
                    elif first == 4:
                        ins.then_inc(sig("mod1_full"), 1)
                        freed[item] = (sig("mod1_full"), 1)
                    else:
                        vector_filled(ins, f"mod{first // 4}")
                        freed[item] = (vector_full, len(v_index))

            def turn_modulation(n):
                if n == 1:
                    pe.wait_ge(sig("mod1_rows"), 1)
                else:
                    from_vector(f"mod{n}")
                bank = vector_bank()
                for j in range(4):
                    ins = transpose(bank[:, j * P:(j + 1) * P], mod_rows[:, j * P:(j + 1) * P])
                vector_filled(ins, f"modT{n}")

            from_vector("cT")
            pe.wait_ge(sig("rstd_diag"), 1)
            bank = vector_bank()
            for t, (t0, tn) in enumerate(TOK_TILES):
                ins = pe.matmul(bank[:, t0:t0 + tn], ones[0:tn, :], rstd_diag[0:tn, t, 0:tn],
                                start=True, stop=True)
            vector_filled(ins, "rstd")
            modulate(0, vector_bank(), range(4))
            turn_modulation(0)

            def project(item, col, width, name, last=False, free=True):
                w = slot_ap(item)[:, 0:WIN[item][1] * KT].rearrange("p (k c) -> p k c", k=KT)
                c0 = col - WIN[item][0]
                to_vector = name == "fa"
                bank = vector_bank() if to_vector else scalar_bank()
                for k in range(KT):
                    if name == "q0":
                        pe.wait_ge(sig("hT"), k + 1)
                    ins = pe.matmul(bank[0:width, 0:T], w[:, k, c0:c0 + width], hT[:, k, :],
                                    start=(k == 0), stop=(k == KT - 1))
                if to_vector:
                    vector_filled(ins, name)
                else:
                    scalar_filled(ins, name)
                if last:
                    freed[item] = (scalar_full, len(a_index))

            def query_rows(b):
                if b >= 2:
                    pe.wait_ge(query_free, b - 1)
                ins = pe.matmul(ps[:, 5 + b % 2, :], ident[0:NS, b:b + 1].to_broadcast([NS, P]), q_rows,
                                start=True, stop=True)
                ins.then_inc(query_full, 1)

            arrived(pe, "qa")
            for i in range(4):
                project("qa", QA + i * P, P, f"q{i}", last=(i == 3))
            arrived(pe, "ka")
            project("ka", KA, P, "k0")
            bank = vector_bank()
            from_scalar("q3")
            for i in range(4):
                ins = transpose(bank[0:NS, i * P:(i + 1) * P], qT[:, i, TP:T])
            vector_filled(ins, "q_rows")
            for i in range(1, 4):
                project("ka", KA + i * P, P, f"k{i}", last=(i == 3))
            from_vector("q_rows")
            query_rows(0)
            query_rows(1)
            arrived(pe, "va")
            for i in range(4):
                project("va", VA + i * P, P, f"v{i}", last=(i == 3))
            arrived(pe, "fqk")
            project("fqk", FA, HA, "fa")
            for name, src in (("k", kT), ("v", vT)):
                from_scalar(f"{name}3")
                for t, (t0, tn) in enumerate(TOK_TILES):
                    bank = vector_bank()
                    for i in range(4):
                        ins = transpose(bank[0:tn, i * P:(i + 1) * P], src[:, i, t0:t0 + tn])
                    vector_filled(ins, f"{name}_tok{t}")
            project("fqk", QB, P, "qb0")
            pe.wait_ge(sig("neg_cum"), 1)
            bank = vector_bank()
            for t, (t0, tn) in enumerate(TOK_TILES):
                transpose(bank[0:tn, t * HA:(t + 1) * HA], fT[:, t0:t0 + tn])
            for t in range(2):
                ins = transpose(bank[:, (3 + t) * HA:(4 + t) * HA], neg_cum[0:HA, t * P:(t + 1) * P])
            vector_filled(ins, "f_tok")
            pe.wait_ge(sig("qk_new"), 1)
            bank = vector_bank()
            pe.matmul(bank[:, 0:HA * NS], ones[:, :], qk_new.rearrange("p a b -> p (a b)"), start=True, stop=True)
            ins = pe.matmul(bank[:, HA * NS:2 * HA * NS], ones[0:NS, :], f_diag.rearrange("p a b -> p (a b)"),
                            start=True, stop=True)
            vector_filled(ins, "new")

            def head_scores(h):
                i, half = h // 2, slice(64 * (h % 2), 64 * (h % 2) + 64)
                bank = vector_bank()
                for t in range(2):
                    c0, n = (0, P) if t == 0 else (P, 2 * P)
                    pe.matmul(bank[:, c0:c0 + n], qT[half, i, t * P:(t + 1) * P], kT[half, i, 0:n],
                              start=True, stop=False)
                    row = 64 * (h % 2) + h
                    ins = pe.matmul(bank[:, c0:c0 + n], ident[half, row:row + 1].to_broadcast([64, P]),
                                    neg_cum[half, 0:n], start=False, stop=True)
                vector_filled(ins, f"scores{h}")

            def head_turn(h):
                pe.wait_ge(sig("probs"), h + 1)
                bank = scalar_bank()
                for j in range(3):
                    ins = transpose(bank[:, j * P:(j + 1) * P], attn[:, h % 2, j * P:(j + 1) * P])
                scalar_filled(ins, f"turned{h}")

            pv_bank = [None]

            def head_values(h):
                from_scalar(f"turned{h}")
                if h % 2 == 0:
                    pv_bank[0] = vector_bank()
                half = slice(64 * (h % 2), 64 * (h % 2) + 64)
                out = pv_bank[0][half, :]
                pT = attn[:, 2 + h % 2, :]
                v = v_tok[:, :, h * DH:(h + 1) * DH]
                pe.matmul(out[:, 0:P], v[:, 0, :], pT[:, 0:P], start=True, stop=True)
                pe.matmul(out[:, P:2 * P], v[:, 0, :], pT[:, P:2 * P], start=True, stop=False)
                ins = pe.matmul(out[:, P:2 * P], v[:, 1, :], pT[:, 2 * P:3 * P], start=False, stop=True)
                if h % 2 == 1:
                    vector_filled(ins, f"o{h // 2}")
                else:
                    ins.then_inc(sig("pv_even"), 1)

            from_vector("v_tok1")
            tiles = ([("fqk", QB + P, P, "qb1"), ("fqk", KB, P, "kb0"), ("fqk", KB + P, P, "kb1")]
                     + [("vb", VB + i * P, P, f"vb{i}") for i in range(4)]
                     + [("rb", RB + i * P, P, f"rb{i}") for i in range(4)] + [("rb", ALR, 16, "alr")])
            for s in range(len(tiles)):
                item, col, width, name = tiles[s]
                if s == 0 or tiles[s - 1][0] != item:
                    arrived(pe, item)
                project(item, col, width, name, last=(s + 1 == len(tiles) or tiles[s + 1][0] != item))
                if s < HA:
                    head_scores(s)
                if 1 <= s <= HA:
                    head_turn(s - 1)
                if s % 2 == 1 and 3 <= s < HA + 3:
                    head_values(s - 3)
                    head_values(s - 2)
                if s % 2 == 0 and 2 + s // 2 < NS:
                    query_rows(2 + s // 2)

            from_scalar("alr")
            pe.wait_ge(sig("small_loads"), 32)
            for i in range(2):
                bank = vector_bank()
                vector_filled(pe.matmul(bank[:, 0:T], w_alpha_sb[:, i * P:(i + 1) * P], alrT[:, :],
                                        start=True, stop=True), f"alpha{i}")
            for c in range(NCH):
                bank = scalar_bank()
                for h in range(HB):
                    ins = transpose(bank[0:CH, h * DV:(h + 1) * DV], vbT[:, h, c * CH:(c + 1) * CH])
                scalar_filled(ins, f"vb_tok{c}")
            bank = vector_bank()
            for h in range(HB):
                ins = transpose(bank[0:NS, h * DV:(h + 1) * DV], vbT[:, h, TP:T])
            vector_filled(ins, "vb_rows")
            modulate(4, ps[:, 7, :], [0, 1])
            pe.wait_ge(sig("tri"), 5)
            pe.wait_ge(sig("qg_kg"), 2)
            for i in range(2):
                for f in range(2):
                    half = slice(64 * f, 64 * f + 64)
                    bank = vector_bank()
                    for c in range(NCH):
                        ins = pe.matmul(bank[0:CH, c * CH:(c + 1) * CH], e_k[half, i * NCH + c, :],
                                        e_q[half, i * NCH + c, :], start=True, stop=True)
                    vector_filled(ins, f"A{i}{f}")
            pe.wait_ge(sig("lf_rows"), 16)
            bank = vector_bank()
            for h in range(HA):
                ins = transpose(bank[:, h * 64:(h + 1) * 64], lf_rows[:, h:h + HA * (PAGE - 1) + 1:HA])
            vector_filled(ins, "past_lf")
            modulate(4, ps[:, 7, :], [2])
            pe.wait_ge(sig("kd"), 1)
            for i in range(2):
                bank = scalar_bank()
                for c in range(NCH):
                    ins = transpose(bank[0:CH, c * P:(c + 1) * P], al_d[:, i * NCH + c, :])
                scalar_filled(ins, f"kd_tok{i}")
            from_scalar("kd_tok1")
            for i in range(2):
                for c2 in range(2):
                    bank = vector_bank()
                    for c in (2 * c2, 2 * c2 + 1):
                        ins = pe.matmul(bank[:, (c % 2) * 256:(c % 2) * 256 + 256], kd_tok[:, i, c, :],
                                        vb_tok[:, c, i * 256:(i + 1) * 256], start=True, stop=True)
                    vector_filled(ins, f"kv{i}{c2}")
            modulate(4, ps[:, 7, :], [3])
            pe.wait_ge(sig("qe"), 1)
            from_vector("kv11")
            for h in range(HB):
                i, f = h // 2, h % 2
                bank = vector_bank()
                for c in range(NCH):
                    ins = pe.matmul(bank[:, c * CH:(c + 1) * CH], vb_tok[:, c, h * DV:(h + 1) * DV],
                                    A_T[:, i, f, c * CH:(c + 1) * CH], start=True, stop=(c == 0))
                    if c:
                        ins = pe.matmul(bank[:, c * CH:(c + 1) * CH], gla_S[:, c - 1, i, :],
                                        qe[:, f, i * NCH + c, :], start=False, stop=True)
                vector_filled(ins, f"ob{h}")

            from_vector("past_lf")
            pe.wait_ge(sig("tri"), 5)
            bank = vector_bank()
            vector_filled(pe.matmul(bank[:, :], ones[:, :], past_lf.rearrange("p a b -> p (a b)"),
                                    start=True, stop=True), "page_sums")
            bank = vector_bank()
            vector_filled(pe.matmul(bank[:, :], after[:, :], past_lf.rearrange("p a b -> p (a b)"),
                                    start=True, stop=True), "in_page_suffix")
            gate_tiles = [(item, m) for item in ("ga0", "ga1", "gb0", "gb1") for m in range(4)]

            def gate_tile():
                item, m = gate_tiles.pop(0)
                if m == 0:
                    arrived(pe, item)
                project(item, WIN[item][0] + m * P, P, f"{item}_{m}", last=(m == 3))

            gate_tile()
            turn_modulation(1)
            gate_tile()
            from_vector("vb_rows")
            for b in range(NS):
                if b in (3, 6):
                    gate_tile()
                bank = vector_bank()
                vector_filled(pe.matmul(bank[:, :], ident[0:NS, b:b + 1].to_broadcast([NS, P]), vb_rows,
                                        start=True, stop=True), f"v_row{b}")
            gate_tile()
            from_vector("v_row7")
            state = slot_ap("state")[:, 0:NS * 2 * DV].rearrange("p (b i v) -> p b i v", b=NS, i=2)
            bank = vector_bank()
            out = bank[:, 0:64].rearrange("p (i f b) -> p i f b", i=2, f=2, b=16)[:, :, :, 0:NS]
            for b in range(NS):
                for i in range(2):
                    ins = pe.matmul(out[:, i, :, b], state[:, b, i, :], qb_new[:, i, b, :],
                                    start=True, stop=True)
            vector_filled(ins, "ob_new")
            freed["state"] = (vector_full, len(v_index))
            gate_tile()
            pe.wait_ge(sig("ob_sq"), 1)
            for h in range(HB):
                bank = vector_bank()
                vector_filled(pe.matmul(bank[:, 0:T], ones[:, :], ob_sq[:, h, :], start=True, stop=True),
                              f"ob_ss{h}")

            pe.wait_ge(sig("dec_max"), 1)
            bank = vector_bank()
            vector_filled(transpose(bank[0:64, 0:P], dec_max), "dec_maxT")
            gate_tile()
            pe.wait_ge(sig("dec_diag"), 1)
            bank = vector_bank()
            vector_filled(pe.matmul(bank[:, 0:64], ones[0:64, :], dec_diag, start=True, stop=True), "dec_top")
            gate_tile()
            pe.wait_ge(sig("dec_probs"), 1)
            bank = vector_bank()
            vector_filled(pe.matmul(bank[:, :], ones[:, :], dec_scores[:, :, :].rearrange("p a b -> p (a b)"),
                                    start=True, stop=True), "dec_sums")
            pe.wait_ge(sig("values_cleared"), 1)

            def cached_values(b):
                arrived(pe, f"V{b}")
                pe.wait_ge(sig(f"second_half_V{b}"), 16 * (PAGES // 2))
                if b >= 2:
                    pe.wait_ge(sig("masked"), b - 1)
                v = slot_ap(f"V{b}")[:, 0:PAGES * WA].rearrange("p (j c) -> p j c", j=PAGES)
                for j in range(PAGES):
                    row = 32 * (j % 4)
                    ins = pe.matmul(ps[row:row + HA, 5 + b % 2, :], dec_scores[:, b:HA * NS:NS, j], v[:, j, :],
                                    start=(j < 4), stop=(j >= 4), skip_group_check=True)
                release(ins, f"V{b}")

            def sum_values(b):
                pe.wait_ge(sig("masked"), b + 1)
                pe.matmul(ps[0:NS, 7, :], to_row[:, b, :], masked[:, b % 2, :], start=(b == 0),
                          stop=(b == NS - 1)).then_inc(sig("values_summed"), 1)

            for b in range(NS):
                cached_values(b)
                if b:
                    sum_values(b - 1)
                for _ in range({0: 1, 1: 3, 2: 4}.get(b, 0)):
                    gate_tile()
            sum_values(NS - 1)
            modulate(8, vector_bank(), range(4))
            pe.wait_ge(sig("o_rows"), 1)
            bank = vector_bank()
            for i in range(4):
                ins = transpose(bank[:, i * NS:(i + 1) * NS], o_rows[:, i * P:(i + 1) * P])
            vector_filled(ins, "o_past")
            arrived(pe, "wb0")
            arrived(pe, "wb1")
            pe.wait_ge(sig("oT"), 1)
            wb = [slot_ap(f"wb{n}")[:, 0:4096].rearrange("p (k c) -> p k c", k=4) for n in range(2)]
            for m in range(KT):
                for n, src in enumerate((oT[:, :, :], obT)):
                    bank = vector_bank()
                    for k in range(4):
                        ins = pe.matmul(bank[:, 0:T], wb[n][:, k, m * P:(m + 1) * P], src[:, k, :],
                                        start=(k == 0), stop=(k == 3))
                    vector_filled(ins, f"y{n}_{m}")
                if m == 0:
                    turn_modulation(2)
            freed["wb0"] = freed["wb1"] = (vector_full, len(v_index))
            pe.wait_ge(sig("mixed"), 1)
            arrived(pe, "wo0")
            arrived(pe, "wo1")
            wo = [slot_ap(f"wo{n}")[:, 0:4096].rearrange("p (k c) -> p k c", k=4) for n in range(2)]
            for m in range(KT):
                bank = vector_bank()
                for k in range(KT):
                    ins = pe.matmul(bank[:, 0:T], wo[k // 4][:, k % 4, m * P:(m + 1) * P], hT[:, k, :],
                                    start=(k == 0), stop=(k == KT - 1))
                vector_filled(ins, f"out{m}")
            freed["wo0"] = freed["wo1"] = (vector_full, len(v_index))
            def sum_squares(name, ready):
                bank = vector_bank()
                for k in range(KT):
                    pe.wait_ge(sig(ready), k + 1)
                    ins = pe.matmul(bank[:, 0:T], ones[:, :], sq_zone[:, k, :], start=(k == 0), stop=(k == KT - 1))
                vector_filled(ins, name)

            sum_squares("x1_ss", "x1_sq")
            pe.wait_ge(sig("w_r"), 16)
            bank = vector_bank()
            for k in range(KT):
                pe.wait_ge(sig("h2T"), k + 1)
                ins = pe.matmul(bank[0:NE, 0:T], w_r[:, k, :], hT[:, k, :], start=(k == 0), stop=(k == KT - 1))
            vector_filled(ins, "logitsT")
            from_vector("logitsT")
            bank = vector_bank()
            for t, (t0, tn) in enumerate(TOK_TILES):
                ins = transpose(bank[0:tn, t * NE:(t + 1) * NE], logitsT[:, t0:t0 + tn])
            vector_filled(ins, "logits")
            for t, (t0, tn) in enumerate(TOK_TILES):
                for g in range(2):
                    bank = scalar_bank()
                    for k in range(4):
                        ins = transpose(bank[0:tn, k * P:(k + 1) * P], hT[:, 4 * g + k, t0:t0 + tn])
                    scalar_filled(ins, f"h2_tok{t}{g}")
            pe.wait_ge(sig("chosen"), 1)
            bank = vector_bank()
            for t, (t0, tn) in enumerate(TOK_TILES):
                for u in range(t):
                    pe.matmul(bank[0:tn, t * NE:(t + 1) * NE], ones[:, 0:tn], chosen[:, u, :],
                              start=(u == 0), stop=False)
                pe.matmul(bank[0:tn, t * NE:(t + 1) * NE], before[0:tn, 0:tn], chosen[0:tn, t, :],
                          start=(t == 0), stop=True)
            for t, (t0, tn) in enumerate(TOK_TILES):
                ins = pe.matmul(bank[:, 3 * NE:4 * NE], ones[0:tn, :], chosen[0:tn, t, :],
                                start=(t == 0), stop=(t == 2))
            vector_filled(ins, "places")
            def output_bias():
                pe.wait_ge(sig("gates"), 1)
                for t, (t0, tn) in enumerate(TOK_TILES):
                    ins = transpose(ps[0:NE, 5, t0:t0 + tn], gates[0:tn, t, :])
                ins.then_inc(sig("gates_turned"), 1)
                pe.wait_ge(sig("b_d"), 16)
                pe.wait_ge(sig("gatesT"), 1)
                for m in range(KT):
                    if m >= 2:
                        pe.wait_ge(sig("bias_read"), m - 1)
                    pe.matmul(ps[:, 6 + m % 2, 0:T], b_d_sb[:, m * P:(m + 1) * P], gatesT,
                              start=True, stop=True).then_inc(sig("biased"), 1)

            def gather(n):
                pe.wait_ge(sig("pick_ready"), n + 1)
                for k in range(KT):
                    out = ps[:, 6 + k // 4, (k % 4) * P:(k % 4 + 1) * P]
                    for t, (t0, tn) in enumerate(TOK_TILES):
                        ins = pe.matmul(out, tok[0:tn, t, k * P:(k + 1) * P], pick[0:tn, t, :],
                                        start=(t == 0), stop=(t == 2))
                    if k % 4 == 3:
                        ins.then_inc(sig("gathered"), 1)

            def expert_slot(kind, s, e, edge):
                slot, value = expert_landing(kind, s, e, edge)
                pe.wait_ge(landed[slot], value)
                return ring[:, slot, :]

            def gate_up(n, j, edge, first, between):
                e = 2 * n + j
                if not first:
                    pe.wait_ge(sig("up_clipped"), e - 1)
                banks = ps[:, 2 * j:2 * j + 2, :]
                for c in range(2):
                    for half in range(2):
                        pe.matmul(banks[64 * half:64 * half + CAP, c, :], expert_row[:, j, :],
                                  b_gu_rows[:, half * FF + c * 512:half * FF + (c + 1) * 512],
                                  start=True, stop=False, skip_group_check=True)
                for s in range(4):
                    w = expert_slot("gu", s, e, edge)[:, 0:4096].rearrange("p (k c) -> p k c", k=2)
                    for kk in range(2):
                        k = 2 * s + kk
                        if j == 0 and k % 4 == 0:
                            pe.wait_ge(sig("xg_ready"), 2 * n + 1 + k // 4)
                        for c in range(2):
                            for half in range(2):
                                ins = pe.matmul(banks[64 * half:64 * half + CAP, c, :],
                                                xg[:, k, j * CAP:(j + 1) * CAP],
                                                w[:, kk, half * FF + c * 512:half * FF + (c + 1) * 512],
                                                start=False, stop=(k == KT - 1), skip_group_check=True)
                        if kk == 1:
                            ins.then_inc(sig("slots_used"), 1)
                        else:
                            between(k)

            def turn_hidden(n, j, first):
                pe.wait_ge(sig("hid_ready"), 2 * n + j + 1)
                if not first:
                    pe.wait_ge(sig("turn_read"), 3 * n + j)
                for k in range(KT):
                    ins = pe.matmul(ps[:, 4, k * CAP:(k + 1) * CAP], hid[:, k * P:(k + 1) * P],
                                    ident[0:CAP, 0:CAP], start=True, stop=True)
                ins.then_inc(sig("turned"), 1)

            def turn_put(n):
                pe.wait_ge(sig("put_ready"), n + 1)
                pe.wait_ge(sig("turn_read"), 3 * n + 2)
                for t, (t0, tn) in enumerate(TOK_TILES):
                    ins = transpose(ps[:, 4, t0:t0 + tn], put[0:tn, t, :])
                ins.then_inc(sig("turned"), 1)

            def down(n, j, edge, first):
                e = 2 * n + j
                pe.wait_ge(sig("turn_read"), 3 * n + 1 + j)
                if not first:
                    pe.wait_ge(sig("ye_ready"), e)
                for s in range(2):
                    w = expert_slot("dn", s, e, edge)[:, 0:4096].rearrange("p (k c) -> p k c", k=4)
                    for kk in range(4):
                        k = 4 * s + kk
                        for half in range(2):
                            ins = pe.matmul(ps[64 * half:64 * half + CAP, 5, :], hidT[:, k, :],
                                            w[:, kk, half * 512:(half + 1) * 512],
                                            start=(k == 0), stop=(k == KT - 1), skip_group_check=True)
                    ins.then_inc(sig("slots_used"), 1)

            def combine(n, ms):
                for m in ms:
                    if m == 0:
                        pe.wait_ge(sig("ye_ready"), 2 * n + 2)
                    if m >= 2:
                        pe.wait_ge(sig("added"), n * KT + (m - 1))
                    pe.matmul(ps[:, 6 + m % 2, 0:T], ye_tok[:, m * P:(m + 1) * P], putT,
                              start=True, stop=True).then_inc(sig("combined"), 1)

            def pair(n, first, last, cold):
                def beside_b(k):
                    if not first:
                        combine(n - 1, (k, k + 1))
                    if cold and k == 0:
                        output_bias()
                    if k == 4:
                        turn_hidden(n, 0, cold)

                def beside_next_a(k):
                    if k == 2:
                        turn_hidden(n, 1, False)
                    if k == 6:
                        turn_put(n)

                gate_up(n, 1, False, cold, beside_b)
                if not last:
                    if not first:
                        pe.wait_ge(sig("added"), n * KT)
                    if cold:
                        pe.wait_ge(sig("bias_read"), KT)
                    gather(n + 1)
                down(n, 0, False, cold)
                if not last:
                    gate_up(n + 1, 0, False, False, beside_next_a)
                else:
                    turn_hidden(n, 1, False)
                    turn_put(n)
                down(n, 1, last, False)

            def one_round(rnd):
                n = rnd * PAIRS
                cold = isinstance(rnd, int)
                if not cold:
                    pe.wait_ge(sig("added"), n * KT)
                gather(n)
                gate_up(n, 0, True, cold, lambda k: None)
                pair(n, True, False, cold)
                with pe.Fori(1, PAIRS - 1) as p:
                    pair(n + p, False, False, False)
                pair(n + (PAIRS - 1), False, True, False)
                combine(n + (PAIRS - 1), range(KT))

            pe.wait_ge(sig("b_gu_rows"), 16)
            pe.wait_ge(vector_free, len(v_index))
            pe.wait_ge(scalar_free, len(a_index))
            one_round(0)
            pe.wait_ge(sig("rounds"), 1)
            rounds = pe.value_load(rounds_i[0:1, 0:1], min_val=1, max_val=MAX_ROUNDS)
            with pe.If(rounds > 1):
                with pe.Fori(1, rounds) as rnd:
                    one_round(rnd)

            sum_squares("x2_ss", "x2_sq")
            for g in range(2):
                pe.wait_ge(sig("yT"), 4 * g + 4)
                for t, (t0, tn) in enumerate(TOK_TILES):
                    bank = scalar_bank()
                    for k in range(4):
                        ins = transpose(bank[0:tn, k * P:(k + 1) * P], hT[:, 4 * g + k, t0:t0 + tn])
                    scalar_filled(ins, f"y_tok{t}{g}")

        @block.scalar
        def _(act):
            def dma(out, in_, name):
                act.dma_start(out, in_).then_inc(sig(name), 16)

            def row(vec, n):
                return vec[0].rearrange("(r p) -> r p", p=P)[0:n, :]

            dma(c_rows[0:1, :], c_prompt, "c_rows")
            dma(c_rows[1:9, :], c_sample, "c_rows")
            vectors = {"b_ada": b_ada, "g_mix": g_mix, "g_ffn": g_ffn, "g_gla": g_gla, "b_alpha": b_alpha}
            for name, (r0, n) in VEC_ROWS.items():
                src = row(vectors[name], n) if name != "g_final" else g_final.rearrange("(r p) -> r p", p=P)
                dma(vec_rows[r0:r0 + n, :], src, "vec_rows")
            dma(pages_row[:, :], page_table.rearrange("b (a j) -> a (b j)", a=1), "pages")
            dma(pages_col[:, :], page_table.rearrange("b (j a) -> (b j) a", a=1), "pages")
            dma(w_alpha_sb[:, :], w_alpha[0], "small_loads")
            dma(b_f_col[:, :], b_f[0].rearrange("(h a) -> h a", a=1), "small_loads")

            def take(name):
                act.wait_ge(scalar_full, a_index[name])
                return ps[:, (a_index[name] - 1) % 2, :]

            def copy_out(dst, name, rows=P, cols=T, func=ACT.Copy, scale=1.0):
                bank = take(name)
                src = bank[0:rows, 0:cols]
                if len(dst.shape) == 3:
                    src = src.rearrange("p (a b) -> p a b", b=dst.shape[2])
                nc.scalar.activation(dst, src, func, scale=scale).then_inc(scalar_free, 1)

            def log1p_exp(x, ready, done):
                act.wait_ge(sig(ready), 1)
                nc.scalar.activation(x, x, ACT.Exp).then_inc(sig(ready), 1)
                act.wait_ge(sig(ready), 2)
                nc.scalar.activation(x, x, ACT.Ln, bias=1.0).then_inc(sig(done), 1)

            act.wait_ge(sig("c_rows"), 32)
            nc.scalar.activation(c_rows, c_rows, ACT.Silu).then_inc(sig("c_silu"), 1)
            act.wait_ge(sig("x_tok"), 32)
            act.wait_ge(sig("ssq_ones"), 1)
            for t, (t0, tn) in enumerate(TOK_TILES):
                if t:
                    act.wait_ge(sig("ssq"), t)
                nc.scalar.activation(junk[0:tn, :], tok[0:tn, t, :], ACT.Square,
                                     accum_out=ssq[0:tn, t:t + 1]).then_inc(sig("ssq"), 1)
            act.wait_ge(sig("x_var"), 1)
            nc.scalar.activation(rstd, rstd, ACT.Sqrt).then_inc(sig("x_rms"), 1)
            for i in range(4):
                copy_out(qT[:, i, :], f"q{i}", scale=SCALE)
            for name, dst in (("k", kT), ("v", vT)):
                for i in range(4):
                    copy_out(dst[:, i, :], f"{name}{i}")
            log1p_exp(f_nabs, "f_nabs", "f_log")

            def tile_out(name):
                i = int(name[-1]) if name != "alr" else 0
                if name == "alr":
                    copy_out(alrT, name, rows=16)
                elif name.startswith("qb"):
                    copy_out(qbT[:, i, :], name, scale=DK ** -0.5)
                elif name.startswith("kb"):
                    copy_out(kbT[:, i, :], name)
                elif name.startswith("vb"):
                    copy_out(vbT[:, i, :], name)
                else:
                    copy_out(rbT[:, i, :], name, func=ACT.Silu)

            def head_exp(h):
                act.wait_ge(sig("neg_max"), h + 1)
                sc = attn[:, h % 2, :]
                nc.scalar.activation(sc[:, 0:P], sc[:, 0:P], ACT.Exp, bias=row_max[:, 2 * h:2 * h + 1],
                                     accum_out=row_sum[:, 2 * h:2 * h + 1])
                nc.scalar.activation(sc[:, P:3 * P], sc[:, P:3 * P], ACT.Exp,
                                     bias=row_max[:, 2 * h + 1:2 * h + 2],
                                     accum_out=row_sum[:, 2 * h + 1:2 * h + 2]).then_inc(sig("exps"), 1)

            def head_turned(h):
                if h >= 2 and h % 2 == 0:
                    act.wait_ge(sig("pv_even"), h // 2)
                if h >= 2 and h % 2 == 1:
                    act.wait_ge(vector_full, v_index[f"o{h // 2 - 1}"])
                copy_out(attn[:, 2 + h % 2, :], f"turned{h}", cols=3 * P)

            tile_out("qb0")
            names = ["qb1", "kb0", "kb1"] + [f"vb{i}" for i in range(4)] + [f"rb{i}" for i in range(4)] + ["alr"]
            for s, name in enumerate(names):
                tile_out(name)
                if 1 <= s <= HA:
                    head_turned(s - 1)
                if s < HA:
                    head_exp(s)
            for c in range(NCH):
                copy_out(vb_tok[:, c, :], f"vb_tok{c}", rows=CH, cols=512)
            log1p_exp(al_nabs, "al_nabs", "al_log")
            act.wait_ge(sig("al_d"), 1)
            d = al_d.rearrange("p a b -> p (a b)")
            nc.scalar.activation(e_q.rearrange("p a b -> p (a b)"), d, ACT.Exp).then_inc(sig("al_exp"), 1)
            nc.scalar.activation(e_k.rearrange("p a b -> p (a b)"), d, ACT.Exp, scale=-1.0)\
                .then_inc(sig("al_exp"), 1)
            nc.scalar.activation(e_b.rearrange("p a b -> p (a b)"), al_b.rearrange("p a b -> p (a b)"),
                                 ACT.Exp).then_inc(sig("al_exp"), 1)
            act.wait_ge(sig("la_new"), 1)
            nc.scalar.activation(la_new, la_new, ACT.Exp).then_inc(sig("a_new"), 1)
            act.wait_ge(sig("al_rest"), 1)
            nc.scalar.activation(d, d, ACT.Exp).then_inc(sig("rest_exp"), 1)
            for i in range(2):
                copy_out(kd_tok[:, i, :, :].rearrange("p c k -> p (c k)"), f"kd_tok{i}", rows=CH, cols=512)
            gate_names = [f"{item}_{m}" for item in ("ga0", "ga1", "gb0", "gb1") for m in range(4)]

            def take_gates(n):
                for _ in range(n):
                    name = gate_names.pop(0)
                    dst = gaT if name[1] == "a" else gbT
                    copy_out(dst[:, 4 * int(name[2]) + int(name[4]), :], name, func=ACT.Sigmoid)

            take_gates(6)
            act.wait_ge(vector_free, v_index[f"ob_ss{HB - 1}"])
            nc.scalar.activation(ob_rs, ob_rs, ACT.Sqrt).then_inc(sig("ob_rms"), 1)
            take_gates(2)
            act.wait_ge(sig("dec_shift"), 1)
            nc.scalar.activation(dec_scores[:, :, :], dec_scores[:, :, :], ACT.Exp)
            nc.scalar.activation(s_new, s_new, ACT.Exp).then_inc(sig("dec_probs"), 1)
            take_gates(8)

            def squares_and_root(x_ready, sq_ready, sums, rms_ready):
                for k in range(KT):
                    act.wait_ge(sig(x_ready), k + 1)
                    nc.scalar.activation(sq_zone[:, k, :], xT[:, k, :], ACT.Square).then_inc(sig(sq_ready), 1)
                act.wait_ge(vector_free, v_index[sums])
                nc.scalar.activation(row_t, row_t, ACT.Sqrt).then_inc(sig(rms_ready), 1)

            squares_and_root("x1", "x1_sq", "x1_ss", "x1_rms")
            for t, (t0, tn) in enumerate(TOK_TILES):
                for g in range(2):
                    copy_out(tok[0:tn, t, g * 512:(g + 1) * 512], f"h2_tok{t}{g}", rows=tn, cols=512)
            act.wait_ge(sig("top_shift"), 1)
            nc.scalar.activation(logits, logits, ACT.Exp).then_inc(sig("top_exp"), 1)

            def take_gathered(n):
                for g in range(2):
                    act.wait_ge(sig("gathered"), 2 * n + g + 1)
                    nc.scalar.activation(xg[:, 4 * g:4 * g + 4, :].rearrange("p a b -> p (a b)"),
                                         ps[:, 6 + g, :], ACT.Copy).then_inc(sig("xg_ready"), 1)

            def sigmoid(n, j):
                act.wait_ge(sig("gate_ready"), 2 * n + j + 1)
                nc.scalar.activation(sig_v, gate_v, ACT.Sigmoid, scale=ALPHA).then_inc(sig("sig_ready"), 1)

            def take_hidden(n, j):
                act.wait_ge(sig("turned"), 3 * n + 1 + j)
                nc.scalar.activation(hidT, ps[:, 4, :].rearrange("p (k c) -> p k c", c=CAP), ACT.Copy)\
                    .then_inc(sig("turn_read"), 1)

            def take_put(n):
                act.wait_ge(sig("turned"), 3 * n + 3)
                nc.scalar.activation(putT, ps[:, 4, 0:T], ACT.Copy).then_inc(sig("turn_read"), 1)

            def take_output(n, j, last):
                act.wait_ge(sig("slots_used"), down_done(n, j, last))
                for half in range(2):
                    ins = nc.scalar.activation(ye_tok[64 * j:64 * j + CAP, half * 512:(half + 1) * 512],
                                               ps[64 * half:64 * half + CAP, 5, :], ACT.Copy)
                ins.then_inc(sig("ye_ready"), 1)

            def pair(n, first, last):
                take_hidden(n, 0)
                sigmoid(n, 1)
                if not last:
                    take_gathered(n + 1)
                if not first:
                    act.wait_ge(sig("combined"), n * KT)
                take_output(n, 0, False)
                take_hidden(n, 1)
                take_put(n)
                if not last:
                    sigmoid(n + 1, 0)
                take_output(n, 1, last)

            def one_round(rnd):
                n = rnd * PAIRS
                if not isinstance(rnd, int):
                    act.wait_ge(sig("combined"), n * KT)
                take_gathered(n)
                sigmoid(n, 0)
                pair(n, True, False)
                with act.Fori(1, PAIRS - 1) as p:
                    pair(n + p, False, False)
                pair(n + (PAIRS - 1), False, True)

            one_round(0)
            act.wait_ge(sig("rounds"), 1)
            rounds = act.value_load(rounds_i[0:1, 0:1], min_val=1, max_val=MAX_ROUNDS)
            with act.If(rounds > 1):
                with act.Fori(1, rounds) as rnd:
                    one_round(rnd)
            squares_and_root("x2", "x2_sq", "x2_ss", "x2_rms")
            for g in range(2):
                for t, (t0, tn) in enumerate(TOK_TILES):
                    copy_out(tok[0:tn, t, g * 512:(g + 1) * 512], f"y_tok{t}{g}", rows=tn, cols=512)

        @block.vector
        def _(dve):
            steps = [0]

            def chain(ins):
                steps[0] += 1
                ins.then_inc(vstep, 1)
                dve.wait_ge(vstep, steps[0])

            def take(name):
                dve.wait_ge(vector_full, v_index[name])
                return ps[:, 2 + (v_index[name] - 1) % 3, :]

            def give(ins, name, then_read=False):
                ins.then_inc(vector_free, 1)
                if then_read:
                    dve.wait_ge(vector_free, v_index[name])

            V = nc.vector
            vec = {name: vecT[:, r0:r0 + n] for name, (r0, n) in VEC_ROWS.items()}

            def across(ap, n):
                return ap.unsqueeze(2).to_broadcast([ap.shape[0], ap.shape[1], n])

            V.memset(ssq, 1.0).then_inc(sig("ssq_ones"), 1)
            V.memset(qk_new, 0.0)
            V.memset(qb_new, 0.0)
            V.memset(vecT[:, :], 0.0)
            V.memset(cT[:, :, :], 0.0)
            V.memset(to_row, 0.0)
            chain(V.memset(neg_cum[:, :], 0.0))
            V.memset(to_row.rearrange("p a b -> p (a b)")[:, 0:NS * NS:NS + 1], 1.0)
            give(V.tensor_copy(vecT[:, :], take("vectors")[:, 0:N_VEC]), "vectors")
            give(V.tensor_copy(cT[:, :, 0:9], take("cT")[:, 0:9 * KT].rearrange("p (k c) -> p k c", c=9)), "cT")
            for k in range(KT):
                give(V.tensor_copy(xT[:, k, :], take(f"xT{k}")[:, 0:T]), f"xT{k}")
            dve.wait_ge(sig("ssq"), 3)
            V.tensor_scalar(rstd, ssq, 1.0 / D, EPS, ALU.mult, ALU.add).then_inc(sig("x_var"), 1)
            dve.wait_ge(sig("x_rms"), 1)
            chain(V.reciprocal(rstd, rstd))
            dve.wait_ge(sig("ident"), 1)
            V.tensor_reduce(head_of_row, ident[:, :].rearrange("p (q h) -> p h q", h=32)[:, 0:HA, :], AX_X, ALU.add)
            for t in range(3):
                ins = V.tensor_scalar(rstd_diag[:, t, :], ident[:, :], rstd[:, t:t + 1], None, ALU.mult)
            ins.then_inc(sig("rstd_diag"), 1)

            def modulation_rows(n):
                give(V.tensor_copy(mod_rows, take(f"mod{n}")), f"mod{n}")

            def modulation(n):
                bank = take(f"modT{n}")
                b = vec["b_ada"][:, 16 * n:16 * n + 16].rearrange("p (q j) -> p q j", j=4)
                give(V.tensor_tensor(modT[:, 16 * n:16 * n + 16, :].rearrange("p (q j) c -> p q j c", j=4),
                                     bank.rearrange("p (j q c) -> p q j c", j=4, q=4)[:, :, :, 0:9],
                                     b.unsqueeze(3).to_broadcast([P, 4, 4, 9]), ALU.add),
                     f"modT{n}", then_read=True)

            def normed(gain, shift, g, scale, done):
                V.scalar_tensor_tensor(out=gain[:, :, :], in0=modT[:, scale:scale + KT, :], scalar=1.0,
                                       in1=across(vec[g], 9), op0=ALU.add, op1=ALU.mult)
                chain(V.tensor_tensor(hT[:, :, TP:T], xT[:, :, TP:T],
                                      row_t[:, TP:T].unsqueeze(1).to_broadcast([P, KT, NS]), ALU.mult))
                chain(V.tensor_tensor(hT[:, :, TP:T], hT[:, :, TP:T], gain[:, :, 1:9], ALU.mult))
                V.tensor_tensor(hT[:, :, TP:T], hT[:, :, TP:T], modT[:, shift:shift + KT, 1:9], ALU.add)
                for k in range(KT + 1):
                    if k < KT:
                        V.scalar_tensor_tensor(out=hT[:, k, 0:TP], in0=xT[:, k, 0:TP], scalar=gain[:, k, 0:1],
                                               in1=row_t[:, 0:TP], op0=ALU.mult, op1=ALU.mult)\
                            .then_inc(sig(done + "_scaled"), 1)
                    if k:
                        dve.wait_ge(sig(done + "_scaled"), k)
                        V.tensor_scalar(hT[:, k - 1, 0:TP], hT[:, k - 1, 0:TP], modT[:, shift + k - 1, 0:1], None,
                                        ALU.add).then_inc(sig(done), 1)

            give(V.tensor_copy(row_t, take("rstd")[:, 0:T]), "rstd", then_read=True)
            modulation_rows(0)
            modulation(0)
            normed(gain1, 0, "g_mix", KT, "hT")

            def keys_half(b, part_no):
                if part_no == 0:
                    arrived(dve, f"K{b}")
                    dve.wait_ge(query_full, b + 1)
                n = PAGES // 2
                kc = slot_ap(f"K{b}")[:, part_no * n * WA:(part_no + 1) * n * WA]\
                    .rearrange("p (j c) -> p j c", c=WA)
                ins = V.tensor_tensor(kc, kc, ps[:, 5 + b % 2, :].unsqueeze(1).to_broadcast([P, n, WA]), ALU.mult)
                if part_no == 1:
                    ins.then_inc(query_free, 1)
                    dve.wait_ge(query_free, b + 1)
                else:
                    chain(ins)
                V.tensor_reduce(dec_scores[:, b:HA * NS:NS, part_no * n:(part_no + 1) * n]
                                .rearrange("p h j -> p j h"),
                                kc.rearrange("p j (h d) -> p j h d", d=DH), AX_X, ALU.add)\
                    .then_inc(keys_used, 1)

            give(V.tensor_copy(q_rows, take("q_rows")[0:NS, :]), "q_rows")
            dve.wait_ge(scalar_free, a_index["k3"])
            qk = qk_new.rearrange("p (i f) b -> p i f b", f=2)
            for f in range(2):
                half = slice(64 * f, 64 * f + 64)
                ins = V.tensor_tensor(qk[half, :, f, :], qT[half, :, TP:T], kT[half, :, TP:T], ALU.mult)
            ins.then_inc(sig("qk_new"), 1)
            for b in range(2):
                for part_no in range(2):
                    keys_half(b, part_no)
            dve.wait_ge(sig("small_loads"), 32)
            give(V.tensor_scalar(fT, take("fa")[0:HA, 0:T], b_f_col[:, 0:1], None, ALU.add), "fa",
                 then_read=True)
            V.scalar_tensor_tensor(out=f_nabs, in0=fT, scalar=-1.0, in1=fT, op0=ALU.mult, op1=ALU.min)\
                .then_inc(sig("f_nabs"), 1)
            V.tensor_scalar(fT, fT, 0.0, None, ALU.min)
            for name, dst in (("k", k_tok), ("v", v_tok)):
                for t, (t0, tn) in enumerate(TOK_TILES):
                    out = dst[:, t, :] if t < 2 else k_new_rows if name == "k" else v_new_rows
                    give(V.tensor_copy(out, take(f"{name}_tok{t}")[0:tn, :]), f"{name}_tok{t}")
            dve.wait_ge(sig("f_log"), 1)
            chain(V.tensor_tensor(fT, fT, f_nabs, ALU.subtract))
            chain(V.tensor_tensor_scan(neg_cum[0:HA, 0:TP], ones[0:HA, 0:1].to_broadcast([HA, TP]), fT[:, 0:TP],
                                       0.0, ALU.mult, ALU.subtract))
            V.tensor_copy(neg_cum[64:64 + HA, 0:TP], neg_cum[0:HA, 0:TP])
            V.tensor_tensor(f_diag, across(ident[0:HA, 0:HA], NS),
                            fT[:, TP:T].unsqueeze(1).to_broadcast([HA, HA, NS]), ALU.mult)\
                .then_inc(sig("neg_cum"), 1)
            bank = take("f_tok")
            V.tensor_copy(f_tok[:, 0:2, :], bank[:, 0:2 * HA].rearrange("p (t h) -> p t h", h=HA))
            V.tensor_copy(f_tok[0:NS, 2, :], bank[0:NS, 2 * HA:3 * HA])
            give(V.tensor_copy(f_tok[:, 3:5, :], bank[:, 3 * HA:5 * HA].rearrange("p (t h) -> p t h", h=HA)),
                 "f_tok", then_read=True)
            bank = take("new")
            V.tensor_copy(s_new, bank[:, 0:64].rearrange("p (h b) -> p h b", b=NS))
            give(V.tensor_copy(f_new, bank[:, 64:128].rearrange("p (h b) -> p h b", b=NS)), "new")
            dve.wait_ge(sig("tri"), 5)

            def head_mask(h):
                bank = take(f"scores{h}")
                if h >= 2:
                    dve.wait_ge(scalar_full, a_index[f"turned{h - 2}"])
                sc = attn[:, h % 2, :]
                V.scalar_tensor_tensor(out=sc[:, 0:P], in0=bank[:, 0:P], scalar=f_tok[:, 3, h:h + 1],
                                       in1=causal[:, P:2 * P], op0=ALU.subtract, op1=ALU.add)
                give(V.scalar_tensor_tensor(out=sc[:, P:3 * P], in0=bank[:, P:3 * P], scalar=f_tok[:, 4, h:h + 1],
                                            in1=causal[:, :], op0=ALU.subtract, op1=ALU.add),
                     f"scores{h}", then_read=True)
                V.tensor_reduce(row_max[:, 2 * h:2 * h + 1], sc[:, 0:P], AX_X, ALU.max)
                chain(V.tensor_reduce(row_max[:, 2 * h + 1:2 * h + 2], sc[:, P:3 * P], AX_X, ALU.max))
                V.tensor_scalar(row_max[:, 2 * h:2 * h + 2], row_max[:, 2 * h:2 * h + 2], -1.0, None, ALU.mult)\
                    .then_inc(sig("neg_max"), 1)

            def head_norm(h):
                dve.wait_ge(sig("exps"), h + 1)
                sc = attn[:, h % 2, :]
                chain(V.reciprocal(row_inv[:, 2 * h:2 * h + 2], row_sum[:, 2 * h:2 * h + 2]))
                V.tensor_scalar(sc[:, 0:P], sc[:, 0:P], row_inv[:, 2 * h:2 * h + 1], None, ALU.mult)
                V.tensor_scalar(sc[:, P:3 * P], sc[:, P:3 * P], row_inv[:, 2 * h + 1:2 * h + 2], None,
                                ALU.mult).then_inc(sig("probs"), 1)

            for s in range(12):
                if s < HA:
                    head_mask(s)
                if s % 2 == 1 and 3 <= s < HA + 3:
                    i = (s - 3) // 2
                    give(V.tensor_copy(oT[:, i, 0:TP], take(f"o{i}")[:, 0:TP]), f"o{i}")
                if s < HA:
                    head_norm(s)
                if s < 10:
                    keys_half(2 + s // 2, s % 2)

            for i in range(2):
                give(V.tensor_scalar(al_x[:, i, :], take(f"alpha{i}")[:, 0:T], vec["b_alpha"][:, i:i + 1], None,
                                     ALU.add), f"alpha{i}", then_read=True)
            V.scalar_tensor_tensor(out=al_nabs, in0=al_x, scalar=-1.0, in1=al_x, op0=ALU.mult, op1=ALU.min)\
                .then_inc(sig("al_nabs"), 1)
            chain(V.tensor_scalar(al_x, al_x, 0.0, None, ALU.min))
            give(V.tensor_copy(vb_rows, take("vb_rows")[0:NS, :]), "vb_rows")
            dve.wait_ge(sig("al_log"), 1)
            chain(V.tensor_tensor(al_x, al_x, al_nabs, ALU.subtract))
            V.tensor_scalar(la_new, al_x[:, :, TP:T], 1.0 / TAU, None, ALU.mult).then_inc(sig("la_new"), 1)
            chain(V.tensor_scalar(e_q.rearrange("p (i c) t -> p i (c t)", i=2), al_x[:, :, 0:TP], 1.0 / TAU, None,
                                  ALU.mult))
            for ic in range(2 * NCH):
                ins = V.tensor_tensor_scan(al_b[:, ic, :], ones[:, 0:CH], e_q[:, ic, :], 0.0, ALU.mult, ALU.add)
            chain(ins)
            chain(V.tensor_tensor(al_d, al_b, al_b[:, :, CH // 2 - 1:CH // 2].to_broadcast([P, 2 * NCH, CH]),
                                  ALU.subtract))
            V.tensor_scalar(al_d, al_d, EXP_CLAMP, -EXP_CLAMP, ALU.min, ALU.max).then_inc(sig("al_d"), 1)
            qb_p = qbT[:, :, 0:TP].rearrange("p i (c t) -> p i c t", t=CH)
            kb_p = kbT[:, :, 0:TP].rearrange("p i (c t) -> p i c t", t=CH)

            def by_tile(ap):
                return ap.rearrange("p (i c) t -> p i c t", i=2)

            dve.wait_ge(sig("al_exp"), 2)
            V.tensor_tensor(by_tile(e_q), by_tile(e_q), qb_p, ALU.mult).then_inc(sig("qg_kg"), 1)
            V.tensor_tensor(by_tile(e_k), by_tile(e_k), kb_p, ALU.mult).then_inc(sig("qg_kg"), 1)
            V.tensor_tensor(al_d, al_b[:, :, CH - 1:CH].to_broadcast([P, 2 * NCH, CH]), al_b, ALU.subtract)\
                .then_inc(sig("al_rest"), 1)
            chain(V.memset(qe, 0.0))
            dve.wait_ge(sig("al_exp"), 3)
            for f in range(2):
                half = slice(64 * f, 64 * f + 64)
                ins = V.tensor_tensor(qe[half, f, :, :].rearrange("p (i c) t -> p i c t", i=2),
                                      by_tile(e_b[half, :, :]), qb_p[half, :, :, :], ALU.mult)
            ins.then_inc(sig("qe"), 1)
            dve.wait_ge(sig("rest_exp"), 1)
            V.tensor_tensor(by_tile(al_d), by_tile(al_d), kb_p, ALU.mult).then_inc(sig("kd"), 1)
            chain(V.memset(A_T, 0.0))
            keep = keep_s_le_t[:, :].bitcast(U32).unsqueeze(1).to_broadcast([CH, NCH, CH])
            for i in range(2):
                for f in range(2):
                    bank = take(f"A{i}{f}")
                    give(V.copy_predicated(A_T[:, i, f, :].rearrange("p (c t) -> p c t", t=CH), keep,
                                           bank[0:CH, 0:TP].rearrange("p (c t) -> p c t", t=CH)), f"A{i}{f}")
            keys_half(NS - 1, 0)
            give(V.tensor_copy(past_lf, take("past_lf")[:, :].rearrange("p (a j) -> p a j", j=PAGES)), "past_lf",
                 then_read=True)
            for i in range(2):
                for c2 in range(2):
                    bank = take(f"kv{i}{c2}")
                    for c in (2 * c2, 2 * c2 + 1):
                        for f in range(2):
                            half = slice(64 * f, 64 * f + 64)
                            kv = bank[half, (c % 2) * 256 + f * DV:(c % 2) * 256 + (f + 1) * DV]
                            if c == 0:
                                ins = V.tensor_copy(gla_S[half, 0, i, :], kv)
                            else:
                                ins = V.scalar_tensor_tensor(out=gla_S[half, c, i, :], in0=gla_S[half, c - 1, i, :],
                                                             scalar=e_b[half, i * NCH + c, CH - 1:CH], in1=kv,
                                                             op0=ALU.mult, op1=ALU.add)
                        if c % 2 == 0:
                            chain(ins)
                        elif (i, c2) == (1, 1):
                            give(ins, f"kv{i}{c2}")
                        else:
                            give(ins, f"kv{i}{c2}", then_read=True)
            keys_half(NS - 1, 1)
            for b in range(2):
                ins = V.memset(ps[:, 5 + b, :], 0.0)
            ins.then_inc(sig("values_cleared"), 1)
            dve.wait_ge(sig("stored_early"), 16 * 6)
            for h in range(HB):
                give(V.tensor_copy(obT[:, h, 0:TP], take(f"ob{h}")[:, 0:TP]), f"ob{h}")
            dve.wait_ge(sig("mod1_full"), 1)
            V.tensor_copy(mod_rows, ps[:, 7, :]).then_inc(sig("mod1_rows"), 1)
            give(V.tensor_copy(past_suffix, take("page_sums")[:, :].rearrange("p (a j) -> p a j", j=PAGES)),
                 "page_sums", then_read=True)
            for j in range(PAGES - 2, 0, -1):
                chain(V.tensor_tensor(past_suffix[:, :, j:j + 1], past_suffix[:, :, j:j + 1],
                                      past_suffix[:, :, j + 1:j + 2], ALU.add))
            dve.wait_ge(keys_used, 2 * NS)
            ds_ = dec_scores[:, :, :]
            give(V.tensor_tensor(ds_, ds_, take("in_page_suffix")[:, :].rearrange("p (a j) -> p a j", j=PAGES),
                                 ALU.add), "in_page_suffix", then_read=True)
            chain(V.tensor_tensor(ds_[:, :, 0:PAGES - 1], ds_[:, :, 0:PAGES - 1], past_suffix[:, :, 1:PAGES], ALU.add))
            chain(V.tensor_tensor(ds_, ds_, f_new.rearrange("p h b -> p (h b)").unsqueeze(2)
                                  .to_broadcast([P, HA * NS, PAGES]), ALU.add))
            chain(V.tensor_reduce(dec_max, ds_, AX_X, ALU.max))
            V.tensor_tensor(dec_max, dec_max, s_new.rearrange("p h b -> p (h b)"), ALU.max)\
                .then_inc(sig("dec_max"), 1)
            modulation(1)

            state = slot_ap("state")[:, 0:NS * 2 * DV].rearrange("p (b i v) -> p b i v", b=NS, i=2)
            arrived(dve, "state")
            dve.wait_ge(sig("a_new"), 1)
            chain(V.tensor_tensor(state, state, la_new.rearrange("p i b -> p b i").unsqueeze(3)
                                  .to_broadcast([P, NS, 2, DV]), ALU.mult))
            for f in range(2):
                half = slice(64 * f, 64 * f + 64)
                ins = V.tensor_copy(qb_new[half, :, :, f], qbT[half, :, TP:T])
            for b in range(NS):
                bank = take(f"v_row{b}")
                for i in range(2):
                    for f in range(2):
                        half, h = slice(64 * f, 64 * f + 64), 2 * i + f
                        ins = V.scalar_tensor_tensor(out=state[half, b, i, :], in0=bank[half, h * DV:(h + 1) * DV],
                                                     scalar=kbT[half, i, TP + b:TP + b + 1],
                                                     in1=state[half, b, i, :], op0=ALU.mult, op1=ALU.add)
                give(ins, f"v_row{b}")
            bank = take("ob_new")
            give(V.tensor_copy(obT[:, :, TP:T], bank[:, 0:64].rearrange("p (h b) -> p h b", h=4)[:, :, 0:NS]),
                 "ob_new", then_read=True)
            V.tensor_tensor(ob_sq, obT, obT, ALU.mult).then_inc(sig("ob_sq"), 1)
            for h in range(HB):
                give(V.tensor_scalar(ob_rs[:, h, :], take(f"ob_ss{h}")[:, 0:T], 1.0 / DV, EPS, ALU.mult, ALU.add),
                     f"ob_ss{h}", then_read=(h == HB - 1))
            bank = take("dec_maxT")
            give(V.tensor_reduce(dec_m, bank[0:64, 0:P], AX_X, ALU.max), "dec_maxT", then_read=True)
            V.tensor_scalar(dec_diag, ident[0:64, 0:64], dec_m, None, ALU.mult).then_inc(sig("dec_diag"), 1)
            give(V.tensor_copy(dec_top, take("dec_top")[:, 0:64]), "dec_top", then_read=True)
            V.tensor_tensor(ds_, ds_, dec_top.unsqueeze(2).to_broadcast([P, HA * NS, PAGES]), ALU.subtract)
            V.tensor_tensor(s_new, s_new, dec_top.rearrange("p (h b) -> p h b", b=NS), ALU.subtract)\
                .then_inc(sig("dec_shift"), 1)
            dve.wait_ge(sig("ob_rms"), 1)
            chain(V.reciprocal(ob_rs, ob_rs))
            chain(V.tensor_tensor(obT, obT, ob_rs, ALU.mult))
            for h in range(HB):
                ins = V.scalar_tensor_tensor(out=obT[:, h, :], in0=obT[:, h, :], scalar=vec["g_gla"][:, h:h + 1],
                                             in1=rbT[:, h, :], op0=ALU.mult, op1=ALU.mult)
            ins.then_inc(sig("gla_done"), 1)
            bank = take("dec_sums")
            dve.wait_ge(sig("dec_probs"), 1)
            inv = dec_inv.rearrange("p h b -> p (h b)")
            give(V.tensor_reduce(inv, bank[:, :].rearrange("p (a j) -> p a j", j=PAGES), AX_X, ALU.add), "dec_sums",
                 then_read=True)
            chain(V.tensor_tensor(inv, inv, s_new.rearrange("p h b -> p (h b)"), ALU.add))
            chain(V.reciprocal(inv, inv))
            p_new = s_new.rearrange("p (i f) b -> p i f b", f=2)
            inv4 = dec_inv.rearrange("p (i f) b -> p i f b", f=2)
            for f in range(2):
                half = slice(64 * f, 64 * f + 64)
                ins = V.tensor_tensor(o_new[half, :, :], vT[half, :, TP:T], p_new[half, :, f, :], ALU.mult)
            chain(ins)
            for b in range(NS):
                dve.wait_ge(*freed[f"V{b}"])
                V.tensor_tensor(masked[:, b % 2, :].rearrange("p (h d) -> p h d", h=HA),
                                ps[:, 5 + b % 2, :].rearrange("p (h d) -> p h d", h=HA),
                                across(head_of_row, DH), ALU.mult).then_inc(sig("masked"), 1)
            dve.wait_ge(sig("values_summed"), NS)
            V.tensor_copy(o_rows, ps[0:NS, 7, :]).then_inc(sig("o_rows"), 1)
            modulation_rows(2)
            o_past = take("o_past")[:, 0:4 * NS].rearrange("p (i b) -> p i b", b=NS)
            give(V.tensor_tensor(o_new, o_new, o_past, ALU.add), "o_past", then_read=True)
            for f in range(2):
                half = slice(64 * f, 64 * f + 64)
                ins = V.tensor_tensor(oT[half, :, TP:T], o_new[half, :, :], inv4[half, :, f, :], ALU.mult)
            ins.then_inc(sig("oT"), 1)

            dve.wait_ge(scalar_free, a_index["gb1_3"])
            for m in range(KT):
                give(V.tensor_tensor(hT[:, m, :], take(f"y0_{m}")[:, 0:T], gaT[:, m, :], ALU.mult), f"y0_{m}")
                give(V.tensor_tensor(gbT[:, m, :], take(f"y1_{m}")[:, 0:T], gbT[:, m, :], ALU.mult), f"y1_{m}",
                     then_read=True)
                ins = V.tensor_tensor(hT[:, m, :], hT[:, m, :], gbT[:, m, :], ALU.add)
                if m == 0:
                    modulation(2)
            ins.then_inc(sig("mixed"), 1)

            for m in range(KT):
                branch, gate, tmp = take(f"out{m}")[:, 0:T], 16 + m, o_new[:, m % 4, :]
                V.tensor_tensor(tmp, branch[:, TP:T], modT[:, gate, 1:9], ALU.mult)
                give(V.scalar_tensor_tensor(out=xT[:, m, 0:TP], in0=branch[:, 0:TP], scalar=modT[:, gate, 0:1],
                                            in1=xT[:, m, 0:TP], op0=ALU.mult, op1=ALU.add), f"out{m}",
                     then_read=True)
                V.tensor_tensor(xT[:, m, TP:T], xT[:, m, TP:T], tmp, ALU.add).then_inc(sig("x1"), 1)

            def rms_row(name, rms_ready):
                give(V.tensor_scalar(row_t, take(name)[:, 0:T], 1.0 / D, EPS, ALU.mult, ALU.add), name,
                     then_read=True)
                dve.wait_ge(sig(rms_ready), 1)
                chain(V.reciprocal(row_t, row_t))

            rms_row("x1_ss", "x1_rms")
            normed(gain2, 24, "g_ffn", 32, "h2T")

            give(V.tensor_copy(logitsT, take("logitsT")[0:NE, 0:T]), "logitsT")
            chain(V.memset(logits, 0.0))
            bank = take("logits")
            dve.wait_ge(sig("b_r"), 16)
            for t, (t0, tn) in enumerate(TOK_TILES):
                ins = V.tensor_tensor(logits[0:tn, t, :], bank[0:tn, t * NE:(t + 1) * NE], b_r[0:tn, :], ALU.add)
            give(ins, "logits", then_read=True)
            for t in range(3):
                ins = V.max(out=top8[:, t, :], in_=logits[:, t, :])
            chain(ins)
            V.tensor_copy(keys8[:, :, 0:4], top8[:, :, 0:4])
            chain(V.tensor_copy(keys8[:, :, 4:8], top8[:, :, 0:1].to_broadcast([P, 3, 4])))
            for t in range(3):
                ins = V.match_replace(out=rest[:, t, :], in_to_replace=keys8[:, t, :], in_values=logits[:, t, :],
                                      imm_value=NEG)
            chain(ins)
            V.tensor_tensor(chosen, rest, logits, ALU.not_equal).then_inc(sig("chosen"), 1)
            V.tensor_tensor(logits, logits, top8[:, :, 0:1].to_broadcast([P, 3, NE]), ALU.subtract)\
                .then_inc(sig("top_shift"), 1)
            bank = take("places")
            dve.wait_ge(sig("chosen"), 1)
            chain(V.memset(place, 0.0))
            chain(V.tensor_reduce(rounds_f[:, 0:1], bank[:, 3 * NE:4 * NE], AX_X, ALU.max))
            for t, (t0, tn) in enumerate(TOK_TILES):
                ins = V.scalar_tensor_tensor(out=place[0:tn, t, :], in0=bank[0:tn, t * NE:(t + 1) * NE], scalar=1.0,
                                             in1=chosen[0:tn, t, :], op0=ALU.add, op1=ALU.mult)
            give(ins, "places", then_read=True)
            chain(V.tensor_scalar(place, place, -1.0, None, ALU.add))
            def set_pick(n, p):
                for j in range(2):
                    V.tensor_copy(expert_row[:, j, :],
                                  ident[0:NE, bass.ds(2 * p + j, 1)].to_broadcast([NE, CAP]))
                    for t, (t0, tn) in enumerate(TOK_TILES):
                        ins = V.tensor_scalar(pick[0:tn, t, j * CAP:(j + 1) * CAP], slots_iota[0:tn, :],
                                              place[0:tn, t, bass.ds(2 * p + j, 1)], None, ALU.is_equal)
                ins.then_inc(sig("pick_ready"), 1)

            def set_put(n, p):
                for j in range(2):
                    for t, (t0, tn) in enumerate(TOK_TILES):
                        ins = V.tensor_scalar(put[0:tn, t, j * CAP:(j + 1) * CAP], slots_iota[0:tn, :],
                                              place[0:tn, t, bass.ds(2 * p + j, 1)],
                                              gates[0:tn, t, bass.ds(2 * p + j, 1)], ALU.is_equal, ALU.mult)
                ins.then_inc(sig("put_ready"), 1)

            def swiglu(n, j, first):
                e = 2 * n + j
                dve.wait_ge(sig("slots_used"), gu_done(n, j, first))
                V.tensor_scalar(gate_v, ps[0:CAP, 2 * j:2 * j + 2, :].rearrange("p a b -> p (a b)"),
                                LIMIT, None, ALU.min).then_inc(sig("gate_ready"), 1)
                V.tensor_scalar(hid, ps[64:64 + CAP, 2 * j:2 * j + 2, :].rearrange("p a b -> p (a b)"),
                                LIMIT, -LIMIT, ALU.min, ALU.max).then_inc(sig("up_clipped"), 1)
                dve.wait_ge(sig("up_clipped"), e + 1)
                V.scalar_tensor_tensor(out=hid, in0=hid, scalar=1.0, in1=gate_v, op0=ALU.add, op1=ALU.mult)\
                    .then_inc(sig("up_times_gate"), 1)
                dve.wait_ge(sig("up_times_gate"), e + 1)
                dve.wait_ge(sig("sig_ready"), e + 1)
                V.tensor_tensor(hid, hid, sig_v, ALU.mult).then_inc(sig("hid_ready"), 1)

            def add_pair(n):
                for m in range(KT):
                    dve.wait_ge(sig("combined"), n * KT + m + 1)
                    V.tensor_tensor(acc[:, m, :], acc[:, m, :], ps[:, 6 + m % 2, 0:T], ALU.add)\
                        .then_inc(sig("added"), 1)

            def pair(n, p, first, last, cold=False):
                swiglu(n, 0, first)
                if cold:
                    output_bias()
                if not last:
                    dve.wait_ge(sig("slots_used"), n * 12 + 5)
                    set_pick(n + 1, p + 1)
                set_put(n, p)
                if not first:
                    add_pair(n - 1)
                swiglu(n, 1, False)

            def one_round(rnd):
                n = rnd * PAIRS
                if not isinstance(rnd, int):
                    for t, (t0, tn) in enumerate(TOK_TILES):
                        ins = V.tensor_scalar(place[0:tn, t, :], place[0:tn, t, :], float(-CAP), None, ALU.add)
                    ins.then_inc(sig("moved_up"), 1)
                    dve.wait_ge(sig("moved_up"), rnd)
                set_pick(n, 0)
                if isinstance(rnd, int):
                    rounds_and_gates()
                pair(n, 0, True, False, cold=isinstance(rnd, int))
                with dve.Fori(1, PAIRS - 1) as p:
                    pair(n + p, p, False, False)
                pair(n + (PAIRS - 1), PAIRS - 1, False, True)
                add_pair(n + (PAIRS - 1))
                dve.wait_ge(sig("added"), n * KT + PAIRS * KT)

            def rounds_and_gates():
                thresholds = rest[:, 0, 0:MAX_ROUNDS - 1]
                for r in range(1, MAX_ROUNDS):
                    ins = V.tensor_scalar(thresholds[:, r - 1:r], rounds_f[:, 0:1], float(CAP * r), None, ALU.is_gt)
                chain(ins)
                chain(V.tensor_reduce(rounds_f[:, 1:2], thresholds, AX_X, ALU.add))
                V.tensor_scalar(rounds_i[0:1, 0:1], rounds_f[0:1, 1:2], 1.0, None, ALU.add).then_inc(sig("rounds"), 1)
                dve.wait_ge(sig("top_exp"), 1)
                chain(V.tensor_tensor(gates, logits, chosen, ALU.mult))
                chain(V.tensor_reduce(rstd, gates, AX_X, ALU.add))
                chain(V.reciprocal(rstd, rstd))
                V.tensor_tensor(gates, gates, across(rstd, NE), ALU.mult).then_inc(sig("gates"), 1)

            def output_bias():
                dve.wait_ge(sig("gates_turned"), 1)
                V.tensor_copy(gatesT, ps[0:NE, 5, 0:T]).then_inc(sig("gatesT"), 1)
                for m in range(KT):
                    dve.wait_ge(sig("biased"), m + 1)
                    V.tensor_copy(acc[:, m, :], ps[:, 6 + m % 2, 0:T]).then_inc(sig("bias_read"), 1)
                dve.wait_ge(sig("bias_read"), KT)

            one_round(0)
            dve.wait_ge(sig("rounds"), 1)
            rounds = dve.value_load(rounds_i[0:1, 0:1], min_val=1, max_val=MAX_ROUNDS)
            with dve.If(rounds > 1):
                with dve.Fori(1, rounds) as rnd:
                    one_round(rnd)

            chain(V.tensor_tensor(acc[:, :, TP:T], acc[:, :, TP:T], modT[:, 40:40 + KT, 1:9], ALU.mult))
            chain(V.tensor_tensor(xT[:, :, TP:T], xT[:, :, TP:T], acc[:, :, TP:T], ALU.add))
            for m in range(KT):
                V.scalar_tensor_tensor(out=xT[:, m, 0:TP], in0=acc[:, m, 0:TP], scalar=modT[:, 40 + m, 0:1],
                                       in1=xT[:, m, 0:TP], op0=ALU.mult, op1=ALU.add).then_inc(sig("x2"), 1)
            rms_row("x2_ss", "x2_rms")
            for k in range(KT):
                V.scalar_tensor_tensor(out=hT[:, k, :], in0=xT[:, k, :], scalar=vec["g_final"][:, k:k + 1],
                                       in1=row_t, op0=ALU.mult, op1=ALU.mult).then_inc(sig("yT"), 1)

        @block.sync
        def _(sp):
            for b in range(NS):
                freed[f"K{b}"] = (keys_used, 2 * (b + 1))
            loaded_pages = [False]

            def load(item):
                n = ITEMS.index(item)
                if n >= SLOTS:
                    before_ = ITEMS[n - SLOTS]
                    sp.wait_ge(*freed[before_])
                    if before_ == "state":
                        sp.wait_ge(sig("state_stored"), 16)
                s, _ = landing[item]
                dst = ring[:, s, :]
                if item[0:3] == "ada":
                    a = int(item[3:])
                    part_no, kp = a // 4, a % 4
                    sp.dma_start(dst[:, 0:4096].rearrange("p (k c) -> p k c", k=2),
                                 w_ada[0].rearrange("(k p) c -> p k c", p=P)[
                                     :, 2 * kp:2 * kp + 2, part_no * 2048:(part_no + 1) * 2048])\
                        .then_inc(landed[s], 16)
                elif item in WIN:
                    c0, n_cols = WIN[item]
                    sp.dma_start(dst[:, 0:n_cols * KT].rearrange("p (k c) -> p k c", k=KT),
                                 w_in[0].rearrange("(k p) c -> p k c", p=P)[:, :, c0:c0 + n_cols])\
                        .then_inc(landed[s], 16)
                elif item[0] in "KV":
                    b = int(item[1:])
                    if not loaded_pages[0]:
                        sp.wait_ge(sig("pages"), 32)
                        loaded_pages[0] = True
                    for half in range(2 if item[0] == "K" else 1):
                        load_pages(sp, item, half, landed[s])
                elif item == "state":
                    sp.dma_start(dst[:, 0:NS * 2 * DV].rearrange("p (a v) -> p a v", v=DV),
                                 state_gla[0].rearrange("b (i f) k v -> (f k) (b i) v", f=2))\
                        .then_inc(landed[s], 16)
                else:
                    w = w_branch if item[1] == "b" else w_o
                    r = int(item[2:])
                    sp.dma_start(dst[:, 0:4096].rearrange("p (k c) -> p k c", k=4),
                                 w[0].rearrange("(k p) c -> p k c", p=P)[:, 4 * r:4 * r + 4, :])\
                        .then_inc(landed[s], 16)

            def store(dst, src):
                sp.dma_start(dst, src).then_inc(sig("stored_early"), 16)

            for item in ITEMS:
                load(item)
                if item == "ada0":
                    sp.dma_start(tok[:, 0:2, :], x_prompt[0].rearrange("(t p) d -> p t d", p=P))\
                        .then_inc(sig("x_tok"), 16)
                    sp.dma_start(tok[0:NS, 2, :], x_sample.rearrange("b s d -> (b s) d"))\
                        .then_inc(sig("x_tok"), 16)
                    sp.wait_ge(sig("vec_rows"), 16 * len(VEC_ROWS))
                if item == "K2":
                    sp.wait_ge(vector_free, v_index["f_tok"])
                    for src, new, d_p, d_s in ((k_tok, k_new_rows, k_prompt, k_sample),
                                               (v_tok, v_new_rows, v_prompt, v_sample)):
                        store(d_p[0, 0].rearrange("(t p) h d -> p t (h d)", p=P), src[:, 0:2, :])
                        store(d_s[0].rearrange("b s h d -> (b s) (h d)"), new)
                    store(logf_prompt[0, 0].rearrange("(t p) h -> p t h", p=P), f_tok[:, 0:2, :])
                    store(logf_sample[0].rearrange("b s h -> (b s) h"), f_tok[0:NS, 2, :])

            gu = w_gu[0].rearrange("e (k p) c -> e p k c", p=P)
            dn = w_d[0].rearrange("e (k p) c -> e p k c", p=P)

            def load_expert(kind, e, number, edge, phase_one=False):
                for s in range(4 if kind == "gu" else 2):
                    slot, _ = expert_landing(kind, s, 0, edge)
                    if phase_one and number + s < SLOTS:
                        sp.wait_ge(*freed[ITEMS[len(ITEMS) - SLOTS + number + s]])
                    else:
                        sp.wait_ge(sig("slots_used"), number + (s + 1 - SLOTS))
                    if kind == "gu":
                        src, k = gu[bass.ds(e, 1), :, 2 * s:2 * s + 2, :], 2
                    else:
                        src, k = dn[bass.ds(e, 1), :, 4 * s:4 * s + 4, :], 4
                    sp.dma_start(ring[:, slot, 0:4096].rearrange("p (k c) -> p k c", k=k),
                                 src.rearrange("e p k c -> (e p) k c")).then_inc(landed[slot], 16)

            def load_round(rnd):
                start, phase_one = rnd * (SLOTS * NE), isinstance(rnd, int)
                load_expert("gu", 0, start, True, phase_one)
                load_expert("gu", 1, start + 4, False, phase_one)
                load_expert("dn", 0, start + 8, False)
                with sp.Fori(1, NE - 1) as e:
                    load_expert("gu", e + 1, start + e * SLOTS + 4, False)
                    load_expert("dn", e, start + e * SLOTS + 8, False)
                load_expert("dn", NE - 1, start + SLOTS * NE - 2, True)

            load_round(0)
            sp.wait_ge(sig("rounds"), 1)
            rounds = sp.value_load(rounds_i[0:1, 0:1], min_val=1, max_val=MAX_ROUNDS)
            with sp.If(rounds > 1):
                with sp.Fori(1, rounds) as rnd:
                    load_round(rnd)
            for g in range(2):
                cols = slice(g * 512, (g + 1) * 512)
                sp.wait_ge(scalar_free, a_index[f"y_tok1{g}"])
                sp.dma_start(y_prompt[0].rearrange("(t p) d -> p t d", p=P)[:, :, cols], tok[:, 0:2, cols])\
                    .then_inc(sig("stored"), 16)
                sp.wait_ge(scalar_free, a_index[f"y_tok2{g}"])
                sp.dma_start(y_sample.rearrange("b s d -> (b s) d")[:, cols], tok[0:NS, 2, cols])\
                    .then_inc(sig("stored"), 16)
            sp.wait_ge(sig("stored_early"), 16 * 6)
            sp.wait_ge(sig("stored"), 64)

        @block.gpsimd
        def _(pool):
            nc.gpsimd.memset(ident[:, :], 0.0).then_inc(gstep, 1)
            nc.gpsimd.memset(ones[:, :], 1.0).then_inc(sig("ones"), 1)
            nc.gpsimd.memset(causal[:, :], 0.0).then_inc(gstep, 1)
            pool.wait_ge(gstep, 2)
            pool.wait_ge(sig("ones"), 1)
            nc.gpsimd.affine_select(out=ident[:, :], in_=ident[:, :], compare_op=ALU.not_equal, fill=1.0,
                                    base=0, pattern=[[-1, P]], channel_multiplier=1).then_inc(sig("ident"), 1)
            nc.gpsimd.affine_select(out=before[:, :], in_=ones[:, :], compare_op=ALU.is_gt, fill=0.0,
                                    base=0, pattern=[[1, P]], channel_multiplier=-1).then_inc(sig("tri"), 1)
            nc.gpsimd.affine_select(out=after[:, :], in_=ones[:, :], compare_op=ALU.is_gt, fill=0.0,
                                    base=0, pattern=[[-1, P]], channel_multiplier=1).then_inc(sig("tri"), 1)
            nc.gpsimd.affine_select(out=causal[:, P:2 * P], in_=causal[:, P:2 * P], compare_op=ALU.is_ge,
                                    fill=NEG, base=0, pattern=[[-1, P]], channel_multiplier=1)\
                .then_inc(sig("tri"), 1)
            nc.gpsimd.affine_select(out=keep_s_le_t[:, :], in_=ones[0:CH, 0:CH], compare_op=ALU.is_ge,
                                    fill=0.0, base=0, pattern=[[1, CH]], channel_multiplier=-1)\
                .then_inc(sig("tri"), 1)
            nc.gpsimd.iota(slots_iota[:, :], pattern=[[1, CAP]], base=0, channel_multiplier=0,
                           allow_small_or_imprecise_dtypes=True).then_inc(sig("tri"), 1)
            pool.wait_ge(sig("pages"), 32)
            nc.gpsimd.indirect_dma_start(
                out=lf_rows, out_offset=None, in_=cache_logf[0].rearrange("n s h -> n (s h)"),
                in_offset=bass.IndirectOffsetOnAxis(ap=pages_col[:, 0:1].bitcast(U32), axis=0)).then_inc(sig("lf_rows"), 16)
            pool.wait_ge(vector_free, v_index["kv11"])
            for i in range(2):
                nc.gpsimd.dma_start(gla_prompt[0, 0, 2 * i:2 * i + 2].rearrange("f k v -> (f k) v"),
                                    gla_S[:, NCH - 1, i, :]).then_inc(sig("gla_stored"), 16)
            def load_values(item):
                pool.wait_ge(*freed[ITEMS[ITEMS.index(item) - SLOTS]])
                load_pages(pool, item, 1, sig(f"second_half_{item}"))

            for b in (0, 1):
                load_values(f"V{b}")
            pool.wait_ge(vector_free, v_index[f"v_row{NS - 1}"])
            nc.gpsimd.dma_start(gla_sample[0].rearrange("b (i f) k v -> (f k) (b i) v", f=2),
                                slot_ap("state")[:, 0:NS * 2 * DV].rearrange("p (a v) -> p a v", v=DV))\
                .then_inc(sig("state_stored"), 16)
            pool.wait_ge(sig("state_stored"), 16)
            for b in range(2, NS):
                load_values(f"V{b}")
            pool.wait_ge(sig("mixed"), 1)
            nc.gpsimd.dma_start(b_gu_rows, b_gu[0]).then_inc(sig("b_gu_rows"), 16)
            nc.gpsimd.dma_start(w_r, w_router[0].rearrange("(k p) e -> p k e", p=P)).then_inc(sig("w_r"), 16)
            nc.gpsimd.dma_start(b_d_sb, b_d[0]).then_inc(sig("b_d"), 16)
            nc.gpsimd.dma_start(b_r, b_router[0].partition_broadcast(P)).then_inc(sig("b_r"), 16)
            pool.wait_ge(sig("gla_stored"), 32)
            pool.wait_ge(sig("state_stored"), 16)


_INS = ["x_prompt", "x_sample", "c_prompt", "c_sample", "cache_k", "cache_v", "cache_logf", "state_gla",
        "page_table", "g_mix", "g_ffn", "g_final", "w_ada", "b_ada", "w_in", "b_f", "w_alpha", "b_alpha",
        "g_gla", "w_branch", "w_o", "w_router", "b_router", "w_gu", "b_gu", "w_d", "b_d"]
_OUTS = [(1, TP, D), (NS, 1, D), (1, 1, TP, HA, DH), (1, 1, TP, HA, DH), (1, 1, TP, HA), (1, 1, HB, DK, DV),
         (1, NS, 1, HA, DH), (1, NS, 1, HA, DH), (1, NS, 1, HA), (1, NS, HB, DK, DV)]


def kernel(**inputs):
    import concourse.bacc as bacc
    from concourse.bass_utils import run_bass_kernel_spmd

    nc = bacc.Bacc("TRN2", target_bir_lowering=False, num_devices=1)
    arrays, args = {}, []
    for name in _INS:
        a = np.ascontiguousarray(inputs[name])
        arrays[f"in_{name}"] = a
        args.append(nc.dram_tensor(f"in_{name}", a.shape, mybir.dt.from_np(a.dtype), kind="ExternalInput").ap())
    for i, shape in enumerate(_OUTS):
        args.append(nc.dram_tensor(f"out_{i}", shape, F32, kind="ExternalOutput").ap())
    decoder_step(nc, *args)
    r = run_bass_kernel_spmd(nc, [arrays], core_ids=[0])
    return tuple(r.results[0][f"out_{i}"] for i in range(len(_OUTS)))
```
